# Optimizing a Trainium2 kernel written in Bass

```python
import jax, jax.numpy as jnp
from jax import lax
import numpy as np

D_MODEL = 1024
BATCH = 1
SEQ = 256
DEPTH = 2
DEC_BATCH = 8
DEC_SEQ = 1
PAST_LEN = 2048
PAGE_SIZE = 128

D_MIX = D_MODEL
C_CONV = 3 * D_MIX // 8
C_POOL = D_MIX // 4
C_ATT = D_MIX - C_CONV - C_POOL
HEAD_DIM = 64
N_HEADS = C_ATT // HEAD_DIM
CONV_W = 31
POOL_WINDOWS = (2, 4, 8, 16)
N_POOL_GROUPS = 4
POOL_GC = C_POOL // N_POOL_GROUPS
POOL_BUF = 15
DILATIONS = (1, 4, 16)
KEYS_PER_PATTERN = 128
N_PAT = 3
SEG = KEYS_PER_PATTERN + 1
MAX_WINDOW = 2048
ROPE_THETA = 10000.0
EPS = 1e-6
Q_BLOCK = 64
D_IN = 3 * C_CONV + 2 * C_POOL + 4 * C_ATT

kernel_name = "hymba_conv_pool_dilated_decoder_step"

def rms_norm(x, g):
    xf = x.astype(jnp.float32)
    y = xf * lax.rsqrt(jnp.mean(xf * xf, axis=-1, keepdims=True) + EPS)
    return (y * g.astype(jnp.float32)).astype(x.dtype)

def layer_norm(x, g, b):
    xf = x.astype(jnp.float32)
    mu = jnp.mean(xf, axis=-1, keepdims=True)
    xc = xf - mu
    y = xc * lax.rsqrt(jnp.mean(xc * xc, axis=-1, keepdims=True) + EPS)
    return (y * g.astype(jnp.float32) + b.astype(jnp.float32)).astype(x.dtype)

def rope(x, pos):
    half = HEAD_DIM // 2
    inv = ROPE_THETA ** (-jnp.arange(half, dtype=jnp.float32) / half)
    ang = pos.astype(jnp.float32)[:, None] * inv[None, :]
    cos = jnp.cos(ang)[None, :, None, :]
    sin = jnp.sin(ang)[None, :, None, :]
    xf = x.astype(jnp.float32)
    x1, x2 = xf[..., :half], xf[..., half:]
    return jnp.concatenate([x1 * cos - x2 * sin, x2 * cos + x1 * sin], axis=-1).astype(x.dtype)

def dilated_offsets():
    j = jnp.arange(SEG, dtype=jnp.int32)
    return jnp.concatenate([d * j for d in DILATIONS])

def dilated_attend(q, kk, vv, qidx):
    B, Tq = q.shape[0], q.shape[1]
    off = dilated_offsets()
    kidx = qidx[:, None] - off[None, :]
    valid = kidx >= 0
    kidx = jnp.maximum(kidx, 0)
    kg = jnp.take(kk, kidx, axis=1)
    vg = jnp.take(vv, kidx, axis=1)
    s = jnp.einsum('bqhd,bqkhd->bhqk', q, kg, preferred_element_type=jnp.float32) * (HEAD_DIM ** -0.5)
    s = jnp.where(valid[None, None], s, -1e30).reshape(B, N_HEADS, Tq, N_PAT, SEG)
    m = jnp.max(s, axis=-1, keepdims=True)
    p = jnp.exp(s - m)
    l = jnp.sum(p, axis=-1)
    o = jnp.einsum('bhqgk,bqgkhd->bqghd', p,
                   vg.reshape(B, Tq, N_PAT, SEG, N_HEADS, HEAD_DIM).astype(jnp.float32))
    lse = m[..., 0] + jnp.log(l)
    alpha = jax.nn.softmax(lse, axis=-1)
    out = jnp.einsum('bqghd,bhqg->bqhd', o, alpha / l)
    return out.astype(q.dtype)

def dilated_attention(q, kk, vv, n_prev):
    B, T = q.shape[0], q.shape[1]
    if T > Q_BLOCK and T % Q_BLOCK == 0:
        def blk(b):
            start = b * Q_BLOCK
            qb = lax.dynamic_slice_in_dim(q, start, Q_BLOCK, axis=1)
            qidx = n_prev + start + jnp.arange(Q_BLOCK, dtype=jnp.int32)
            return dilated_attend(qb, kk, vv, qidx)
        out = lax.map(blk, jnp.arange(T // Q_BLOCK, dtype=jnp.int32))
        return out.transpose(1, 0, 2, 3, 4).reshape(B, T, N_HEADS, HEAD_DIM)
    return dilated_attend(q, kk, vv, n_prev + jnp.arange(T, dtype=jnp.int32))

def causal_dwconv(u_ext, w, b):
    y = lax.conv_general_dilated(u_ext, w[:, None, :], window_strides=(1,), padding='VALID',
                                 dimension_numbers=('NWC', 'WIO', 'NWC'),
                                 feature_group_count=C_CONV)
    return y + b

def multiscale_pool(xb_ext, start_pos, w_pool, scale):
    B, L, _ = xb_ext.shape
    T = L - POOL_BUF
    xf = xb_ext.astype(jnp.float32).reshape(B, L, N_POOL_GROUPS, POOL_GC)
    cs = jnp.concatenate([jnp.zeros((B, 1, N_POOL_GROUPS, POOL_GC), jnp.float32),
                          jnp.cumsum(xf, axis=1)], axis=1)
    hi = cs[:, POOL_BUF + 1:]
    pos = start_pos + jnp.arange(T, dtype=jnp.int32)
    means = []
    for g, w in enumerate(POOL_WINDOWS):
        lo = cs[:, POOL_BUF + 1 - w: POOL_BUF + 1 - w + T, g]
        cnt = jnp.minimum(pos + 1, w).astype(jnp.float32)[None, :, None]
        means.append((hi[:, :, g] - lo) / cnt)
    pooled = jnp.stack(means, axis=2)
    d = pooled - xf[:, POOL_BUF:]
    y = jnp.einsum('btgc,gcd->btgd', d, w_pool.astype(jnp.float32)).reshape(B, T, C_POOL)
    return (y * scale.astype(jnp.float32)).astype(xb_ext.dtype)

def trunk_layer(x, start_pos, conv_buf, pool_buf, k_buf, v_buf,
                norm_g, w_in, conv_w, conv_b, ln_g, ln_b, pool_w, pool_scale, qn_g, kn_g, w_out):
    B, T, _ = x.shape
    h = rms_norm(x, norm_g)
    proj = jnp.einsum('btd,de->bte', h, w_in)
    widths = [C_CONV, C_CONV, C_CONV, C_POOL, C_POOL, C_ATT, C_ATT, C_ATT, C_ATT]
    cuts = [int(c) for c in np.cumsum(widths)[:-1]]
    a_val, a_glu, a_gate, b_val, b_gate, q, k, v, c_gate = jnp.split(proj, cuts, axis=-1)

    u = a_val * jax.nn.sigmoid(a_glu)
    u_ext = jnp.concatenate([conv_buf, u], axis=1)
    c = layer_norm(causal_dwconv(u_ext, conv_w, conv_b), ln_g, ln_b)
    ya = jax.nn.silu(c) * jax.nn.silu(a_gate)
    new_conv = u_ext[:, -(CONV_W - 1):]

    pb_ext = jnp.concatenate([pool_buf, b_val], axis=1)
    yb = multiscale_pool(pb_ext, start_pos, pool_w, pool_scale) * jax.nn.silu(b_gate)
    new_pool = pb_ext[:, -POOL_BUF:]

    pos = start_pos + jnp.arange(T, dtype=jnp.int32)
    q = rope(rms_norm(q.reshape(B, T, N_HEADS, HEAD_DIM), qn_g), pos)
    k = rope(rms_norm(k.reshape(B, T, N_HEADS, HEAD_DIM), kn_g), pos)
    v = v.reshape(B, T, N_HEADS, HEAD_DIM)
    kk = jnp.concatenate([k_buf, k], axis=1)
    vv = jnp.concatenate([v_buf, v], axis=1)
    o = dilated_attention(q, kk, vv, k_buf.shape[1])
    yc = o.reshape(B, T, C_ATT) * jax.nn.silu(c_gate)
    n_keep = min(MAX_WINDOW, kk.shape[1])
    new_k = kk[:, -n_keep:]
    new_v = vv[:, -n_keep:]

    y = jnp.einsum('bte,ed->btd', jnp.concatenate([ya, yb, yc], axis=-1), w_out)
    return x + y, new_conv, new_pool, new_k, new_v

def setup_inputs(seed: int = 0) -> dict:
    key = jax.random.key(seed)
    ks = jax.random.split(key, 20)
    f32 = jnp.float32
    win_buf = min(MAX_WINDOW, PAST_LEN)
    n = lambda i, shape, s: s * jax.random.normal(ks[i], shape, f32)
    return {
        "x_prompt": n(0, (BATCH, SEQ, D_MODEL), 1.0),
        "x_sample": n(1, (DEC_BATCH, DEC_SEQ, D_MODEL), 1.0),
        "state_conv": n(2, (DEPTH, DEC_BATCH, CONV_W - 1, C_CONV), 0.5),
        "state_pool": n(3, (DEPTH, DEC_BATCH, POOL_BUF, C_POOL), 0.6),
        "cache_k_win": n(4, (DEPTH, DEC_BATCH, win_buf, N_HEADS, HEAD_DIM), 1.0),
        "cache_v_win": n(5, (DEPTH, DEC_BATCH, win_buf, N_HEADS, HEAD_DIM), 0.6),
        "norm_g": 1.0 + n(6, (DEPTH, D_MODEL), 0.05),
        "w_in": n(7, (DEPTH, D_MODEL, D_IN), D_MODEL ** -0.5),
        "conv_w": n(8, (DEPTH, CONV_W, C_CONV), CONV_W ** -0.5),
        "conv_b": n(9, (DEPTH, C_CONV), 0.02),
        "ln_g": 1.0 + n(10, (DEPTH, C_CONV), 0.05),
        "ln_b": n(11, (DEPTH, C_CONV), 0.02),
        "pool_w": n(12, (DEPTH, N_POOL_GROUPS, POOL_GC, POOL_GC), POOL_GC ** -0.5),
        "pool_scale": 1.0 + n(13, (DEPTH, C_POOL), 0.1),
        "q_norm_g": 1.0 + n(14, (DEPTH, HEAD_DIM), 0.05),
        "k_norm_g": 1.0 + n(15, (DEPTH, HEAD_DIM), 0.05),
        "w_out": n(16, (DEPTH, D_MIX, D_MODEL), 0.5 * D_MIX ** -0.5),
    }

def reference(x_prompt, x_sample, state_conv, state_pool, cache_k_win, cache_v_win,
              norm_g, w_in, conv_w, conv_b, ln_g, ln_b, pool_w, pool_scale,
              q_norm_g, k_norm_g, w_out):
    B = x_prompt.shape[0]
    dt = x_prompt.dtype
    xp, xs = x_prompt, x_sample
    pc, pp, pk, pv = [], [], [], []
    sc, sp, sk, sv = [], [], [], []
    for l in range(DEPTH):
        params = (norm_g[l], w_in[l], conv_w[l], conv_b[l], ln_g[l], ln_b[l],
                  pool_w[l], pool_scale[l], q_norm_g[l], k_norm_g[l], w_out[l])
        xp, c1, p1, k1, v1 = trunk_layer(
            xp, 0,
            jnp.zeros((B, CONV_W - 1, C_CONV), dt), jnp.zeros((B, POOL_BUF, C_POOL), dt),
            jnp.zeros((B, 0, N_HEADS, HEAD_DIM), dt), jnp.zeros((B, 0, N_HEADS, HEAD_DIM), dt),
            *params)
        xs, c2, p2, k2, v2 = trunk_layer(
            xs, PAST_LEN, state_conv[l], state_pool[l], cache_k_win[l], cache_v_win[l], *params)
        pc.append(c1); pp.append(p1); pk.append(k1); pv.append(v1)
        sc.append(c2); sp.append(p2); sk.append(k2); sv.append(v2)
    return (xp, xs, jnp.stack(pc), jnp.stack(pp), jnp.stack(pk), jnp.stack(pv),
            jnp.stack(sc), jnp.stack(sp), jnp.stack(sk), jnp.stack(sv))


_drawn_inputs = setup_inputs


def setup_inputs(seed=0):
    import zlib

    import numpy as np

    out = dict(_drawn_inputs(seed))
    spreads = {}
    factors = {'conv_b': 8.0, 'ln_g': 6.088, 'ln_b': 8.0, 'pool_scale': 3.163, 'q_norm_g': 21.592}
    for name, (base, spread) in spreads.items():
        noise = np.random.default_rng([zlib.crc32(name.encode()), seed]).standard_normal(out[name].shape)
        drawn = base * np.exp(spread * noise) if base else spread * noise
        out[name] = __import__('jax').numpy.asarray(drawn.astype(out[name].dtype))
    for name, factor in factors.items():
        out[name] = (out[name] * factor).astype(out[name].dtype)
    return out
```

```python
from contextlib import ExitStack

import numpy as np

import concourse.bass as bass
from concourse import mybir

F32 = mybir.dt.float32
ALU = mybir.AluOpType
ACT = mybir.ActivationFunctionType
AX = mybir.AxisListType

P = 128
DEPTH, D_MODEL, SEQ, NS, PAST = 2, 1024, 256, 8, 2048
C_CONV, C_POOL, C_ATT, HD = 384, 256, 384, 64
NH = C_ATT // HD
CONV_W, POOL_BUF, POOL_WINDOWS = 31, 15, (2, 4, 8, 16)
DILATIONS, KEYS = (1, 4, 16), 128
EPS = 1e-6
D_IN = 3 * C_CONV + 2 * C_POOL + 4 * C_ATT
T = SEQ + NS
KD = D_MODEL // P
CT, PT_, AT = C_CONV // P, C_POOL // P, C_ATT // P
TAIL = CONV_W - 1
PER_S = P // NS
SCALE = float(HD) ** -0.5
MASKED = -1e30

GATHER = []
_hi = PAST
for _d in DILATIONS:
    _lo = PAST - _d * KEYS
    GATHER.append((_lo, _d, (_hi - _lo) // _d // PER_S))
    _hi = _lo
SLOTS = sum(g[2] for g in GATHER)
NEW = SLOTS
SCORE_CUTS = [(0, 7), (7, 14), (14, SLOTS)]

COL = {}
_c = 0
for _n, _w in (("a_val", C_CONV), ("a_glu", C_CONV), ("a_gate", C_CONV), ("b_val", C_POOL), ("b_gate", C_POOL),
               ("q", C_ATT), ("k", C_ATT), ("v", C_ATT), ("c_gate", C_ATT)):
    COL[_n] = _c
    _c += _w

ROW_CW = 0
ROW_CB = CONV_W * CT
ROW_LG = ROW_CB + CT
ROW_LB = ROW_LG + CT
ROW_PS = ROW_LB + CT
ROW_NG = ROW_PS + PT_
ROW_QN = ROW_NG + KD
ROW_KN = ROW_QN + 1
ROWS = ROW_KN + 1

PROJ = [("q", t, "wq", t * P) for t in range(AT)]
PROJ += [("k", t, "wq", C_ATT + t * P) for t in range(AT)]
PROJ += [("v", t, "wq", 2 * C_ATT + t * P) for t in range(AT)]
for _t in range(CT):
    PROJ += [("a_val", _t, "wa", _t * P), ("a_glu", _t, "wa", C_CONV + _t * P)]
PROJ += [("c_gate", t, "wq", 2 * C_POOL + t * P) for t in range(AT)]
PROJ += [("a_gate", t, "wa", 2 * C_CONV + t * P) for t in range(CT)]
PROJ += [("b_val", t, "wq", t * P) for t in range(PT_)]
PROJ += [("b_gate", t, "wq", C_POOL + t * P) for t in range(PT_)]
NPROJ = len(PROJ)
PIDX = {(g, t): n for n, (g, t, _, _) in enumerate(PROJ)}
RING = 3
NRING = NPROJ + KD
assert NRING % RING == 0

SCHEDULE = ["par", "st0", "st1", "rms"]
for _n in range(9):
    SCHEDULE.append(("proj", _n))
    if 1 <= _n <= 6:
        SCHEDULE.append(("norm", _n - 1))
_side = {
    9: [("vtok", 0), "rep"],
    10: [("vtok", 1), ("score", 0)],
    11: ["qb", "kb"],
    12: [("soft", 0), "vb", ("score", 1)],
    13: [("probT", 0), ("ktok", 0), ("sscore", 0)],
    14: [("out", 0), ("soft", 1), ("score", 2), ("conv", 0, 6), ("sscore", 1)],
    15: [("probT", 1), ("ktok", 1), ("conv", 6, 12), "sconv"],
    16: [("out", 1), ("soft", 2), ("score", 3), ("conv", 12, 18), ("sscore", 2)],
    17: [("probT", 2), ("conv", 18, 27), "ssoft0"],
    18: [("out", 2), ("soft", 3), ("score", 4), ("conv", 27, 33), "ssoft1"],
    19: [("probT", 3), ("conv", 33, 42)],
    20: [("out", 3), ("soft", 4), ("score", 5), ("conv", 42, 51), "spv"],
    21: [("probT", 4), ("conv", 51, 60)],
    22: [("out", 4), ("soft", 5), ("conv", 60, 66), "pool"],
    23: [("probT", 5), ("conv", 66, 75)],
    24: [("out", 5), ("conv", 75, 84), "poolw", ("conv", 84, 93)],
}
for _n in range(9, NPROJ):
    SCHEDULE.append(("proj", _n))
    SCHEDULE += _side[_n]
SCHEDULE += ["tails", "ln"] + [("wout", m) for m in range(KD)]

TR = {}
for _s in SCHEDULE:
    if _s in ("par", "st0", "st1", "qb", "kb", "vb") or (isinstance(_s, tuple) and _s[0] in ("vtok", "ktok", "probT")):
        TR[_s] = len(TR)
    if _s == "tails":
        for _x in ("conv_p", "conv_s", "pool_ps"):
            TR[_x] = len(TR)
NTR = len(TR)
ST = {}
for _s in SCHEDULE:
    if _s in ("rms", "spv") or (isinstance(_s, tuple) and _s[0] == "norm"):
        ST[_s] = len(ST)
    if _s == "ln":
        ST["mean"] = len(ST)
        ST["var"] = len(ST)
NST = len(ST)
NRT = 2 * AT + PT_

PAIRS = DEPTH * NS
PAIRS_A, PAIRS_B, PAIRS_C = 2, 2, 2
PAIRS_IN = PAIRS_A + PAIRS_B + PAIRS_C
XROUNDS = 5


def multiplicity(off):
    return sum((off >= 0) & (off % d == 0) & (off <= d * KEYS) for d in DILATIONS)


def constants():
    f = np.float32
    half = HD // 2
    inv = np.power(f(10000.0), -np.arange(half, dtype=f) / f(half)).astype(f)
    pos = np.concatenate([np.arange(SEQ), np.full(NS, PAST)]).astype(f)
    ang = (pos[None, :] * inv[:, None]).astype(f)
    part = np.arange(P)
    cos, sin = np.cos(ang)[part % half].astype(f), np.sin(ang)[part % half].astype(f)
    ident = np.eye(P, dtype=f)
    heads = (part[:, None] // HD == part[None, :] // HD).astype(f)
    rot = np.zeros((P, P), f)
    for m in range(P):
        rot[m + half if m % HD < half else m - half, m] = -1.0 if m % HD < half else 1.0

    def log_of(c):
        return np.where(c > 0, np.log(np.maximum(c, 1)), MASKED).astype(f)

    i, j = part[:, None], np.arange(SEQ)[None, :]
    bias = np.concatenate([log_of(multiplicity(i - j[:, :P])), log_of(multiplicity(P + i - j))], axis=1)
    a = part[:, None] % PER_S
    offs = [PAST - (lo + d * (n * a + np.arange(n)[None, :])) for lo, d, n in GATHER]
    sbias = np.concatenate([log_of(multiplicity(o)) for o in offs]
                           + [log_of(np.where(a == 0, multiplicity(np.zeros_like(a)), 0))], axis=1)
    mask = (part[:, None] // PER_S == np.arange(NS)[None, :]).astype(f)
    win = np.array(POOL_WINDOWS)[np.stack([part // 64, 2 + part // 64], axis=1)]
    cnt = np.minimum(pos[None, None, :] + 1, win[:, :, None])
    inv_cnt = (f(1.0) / cnt.astype(f)).astype(f).reshape(P, -1)
    eps = np.full((P, 1), EPS, f)
    parts = dict(cos=cos, sin=sin, ident=ident, heads=heads, rot=rot, ones=np.ones((P, P), f), bias=bias,
                 sbias=sbias, mask=mask, inv_cnt=inv_cnt, eps=eps)
    at, n = {}, 0
    for name, v in parts.items():
        at[name] = (n, n + v.shape[1])
        n += v.shape[1]
    return at, np.ascontiguousarray(np.concatenate(list(parts.values()), axis=1))


def trunk_program(nc, ins, const, const_at, outs):
    (y_prompt, y_sample, o_conv_p, o_pool_p, o_k_p, o_v_p, o_conv_s, o_pool_s, o_k_s, o_v_s) = outs
    with ExitStack() as ctx:
        def sb(name, shape):
            return ctx.enter_context(nc.sbuf_tensor(name, shape, F32))

        def bank(name):
            return ctx.enter_context(nc.psum_tensor(name, [P, 512], F32))

        def sem(name):
            return ctx.enter_context(nc.semaphore(name))

        cst = sb("cst", [P, const.shape[1]])
        C = {name: cst[:, a:b] for name, (a, b) in const_at.items()}
        wq = sb("wq", [P, KD, 3 * C_ATT])
        wa = sb("wa", [P, KD, 3 * C_CONV])
        wbuf = {"wq": wq, "wa": wa}
        kv = sb("kv", [P, SLOTS, C_ATT])
        x_tok = kv[:, :, :].rearrange("p a b -> p (a b)")
        xT = sb("xT", [P, KD, T])
        hT = sb("hT", [P, KD, T])
        mix = sb("mix", [P, KD, T])
        prow = sb("prow", [ROWS, P])
        par = sb("par", [P, ROWS])
        cw = par[:, ROW_CW:ROW_CB].rearrange("p (w t) -> p t w", t=CT)
        r_h = sb("r_h", [P, T])
        sq = sb("sq", [P, 2, T])
        qg = sb("qg", [P, 2, T])
        r_qk = sb("r_qk", [P, 2, T])
        roped = sb("roped", [P, T])
        ropes = sb("ropes", [P, T])
        qk = sb("qk", [P, 2 * AT, T])
        vT = sb("vT", [P, AT, T])
        v_tok = sb("v_tok", [P, 2, C_ATT])
        k_tok = sb("k_tok", [P, 2, C_ATT])
        qb = sb("qb", [P, C_ATT])
        kvb = sb("kvb", [P, 2, C_ATT])
        rep = sb("rep", [P, 3, AT, P])
        prod = sb("prod", [P, C_ATT])
        ssc = sb("ssc", [P, SLOTS + 1, NH])
        spr = sb("spr", [P, SLOTS + 1, NH])
        spm = sb("spm", [P, (SLOTS + 1) * NH, NS])
        spsum = sb("spsum", [P, NH * NS])
        srl = sb("srl", [P, NH * NS])
        so = sb("so", [P, AT, 2, NS])
        mx = sb("mx", [P, 4, 32])
        mx2 = sb("mx2", [P, 2])
        u_ext = sb("u_ext", [P, CT, TAIL + SEQ])
        u_smp = sb("u_smp", [P, CT, NS, CONV_W])
        uw = sb("uw", [P, NS, CONV_W])
        yc = sb("yc", [P, CT, T])
        sig_a = sb("sig_a", [P, CT, T])
        sig_b = sb("sig_b", [P, PT_, T])
        sig_c = sb("sig_c", [P, AT, T])
        ex = sb("ex", [P, 2, T])
        p_ext = sb("p_ext", [P, PT_, POOL_BUF + SEQ])
        p_smp = sb("p_smp", [P, PT_, NS, POOL_BUF + 1])
        pa = sb("pa", [P, POOL_BUF + SEQ])
        pb = sb("pb", [P, POOL_BUF + SEQ])
        pd = sb("pd", [P, PT_, T])
        pw = sb("pw", [P, PT_, P])
        sc = sb("sc", [P, 2, 3 * P])
        nmax = sb("nmax", [P, 2, 2])
        lsum = sb("lsum", [P, 2, 2])
        rl = sb("rl", [P, 2, 2])
        pT = sb("pT", [P, 2, 3 * P])
        st_conv = sb("st_conv", [NS * TAIL // 2, 2, C_CONV])
        st_pool = sb("st_pool", [NS * POOL_BUF, C_POOL])
        t_conv_p = sb("t_conv_p", [TAIL, C_CONV])
        t_conv_s = sb("t_conv_s", [NS, C_CONV])
        t_pool_p = sb("t_pool_p", [POOL_BUF, C_POOL])
        t_pool_s = sb("t_pool_s", [NS, C_POOL])

        pj = [bank(f"pj{i}") for i in range(RING)]
        ps = bank("ps")
        prt = bank("prt")
        psc = bank("psc")
        ptr = bank("ptr")
        po = bank("po")

        per = {}

        def counted(name, n):
            s = sem(name)
            per[name] = n
            return s, name

        S = {}
        for name, n in dict(
                par_in=10 * 16, st_in=2 * 16, pw_in=4 * 16, wq_q=16, wq_k=16, wq_v=16, wq_b=16, wq_c=16,
                wa_val=16, wa_glu=16, wa_gate=16, wo_0=16, wo_1=16, k_in=3 * NS * 16, v_in=3 * NS * 16,
                v_out=16, k_out=16, new_out=2 * 16, tail_out=4 * 16, state_out=2 * 16,
                pj_full=NRING, pj_free0=NRING // RING, pj_free1=NRING // RING, pj_free2=NRING // RING,
                tr_full=NTR, tr_free=NTR, st_full=NST, st_free=NST, rt_full=NRT, rt_free=NRT,
                sc_full=NH, sc_free=NH, o_full=NH, o_free=AT,
                xsq=1, r_h_ok=1, h_ok=1, qk_raw=2 * AT, qk_r=2 * AT, qk_ok=2 * AT,
                v_raw=AT, rep_ok=3, exp_ok=CT + AT + CT + PT_, u_ok=CT, sig_c_ok=AT, sig_a_ok=CT, sig_b_ok=PT_,
                nmax_ok=NH, p_raw=NH, p_ok=NH, ks_used=1, ssub=1, sexp=1, spm_ok=1, conv_ok=93, yc_ok=1,
                ysq=1, rstd_ok=1, z_ok=1, zexp=1, b_val_ok=PT_, pd_ok=1,
                mix_a=1, mix_b=PT_, mix_c=AT, mix_s=1, xT_ok=KD).items():
            S[name] = sem(name)
            per[name] = n
        const_in, x_in = sem("const_in"), sem("x_in")
        bulk_out, y_out = sem("bulk_out"), sem("y_out")
        zeroed, x_turned, x_copied = sem("zeroed"), sem("x_turned"), sem("x_copied")
        y_turned, y_copied = sem("y_turned"), sem("y_copied")
        dve_done = sem("dve_done")

        block = ctx.enter_context(nc.Block())

        START = ("pj_free0", "pj_free1", "pj_free2", "tr_free", "st_free", "rt_free", "sc_free", "o_free")
        STAGED = {"v_staged": "v_out", "k_staged": "k_out", "new_staged": "new_out", "tail_staged": "tail_out"}
        for name in STAGED:
            S[name] = sem(name)
            per[name] = 1
        first = {name: 1 for name in (*START, *STAGED, "xT_ok")}

        def nth(l, name, n):
            return l * per[name] + n + first.get(name, 0)

        cache = {"k": ins["cache_k_win"], "v": ins["cache_v_win"]}

        @block.sync
        def _(sp):
            sp.dma_start(x_tok[:, 0:2 * D_MODEL].rearrange("p (r d) -> p r d", r=2),
                         ins["x_prompt"].rearrange("b (r p) d -> p (b r) d", p=P)).then_inc(x_in, 16)
            sp.dma_start(x_tok[0:NS, 2 * D_MODEL:3 * D_MODEL],
                         ins["x_sample"].rearrange("s t d -> (s t) d")).then_inc(x_in, 16)
            sp.dma_start(cst[:, :], const).then_inc(const_in, 16)

            def bulk_pairs(first, count):
                n = (PAST - 1) * C_ATT
                with sp.Fori(0, count) as i:
                    for kind, out in (("k", o_k_s), ("v", o_v_s)):
                        src = cache[kind].rearrange("l s t h d -> (l s) (t h d)")[bass.ds(first + i, 1)]
                        dst = out.rearrange("l s t h d -> (l s) (t h d)")[bass.ds(first + i, 1)]
                        sp.dma_start(dst[:, 0:n].rearrange("o (c e f) -> (o c) e f", c=16, f=PAST - 1),
                                     src[:, C_ATT:].rearrange("o (c e f) -> (o c) e f", c=16, f=PAST - 1))\
                            .then_inc(bulk_out, 16)

            def one(name, l):
                return ins[name][bass.ds(l, 1)]

            def gather(kind, l, name):
                at = 0
                for lo, d, n in GATHER:
                    for s in range(NS):
                        rows = one(f"cache_{kind}_win", l)[:, s, lo:lo + d * n * PER_S]
                        rows = rows.rearrange("o (a b e) h d -> (o a) b e (h d)", a=PER_S, e=d)[:, :, 0, :]
                        sp.dma_start(kv[s * PER_S:(s + 1) * PER_S, at:at + n, :], rows).then_inc(S[name], 16)
                    at += n

            def weights(l, buf, at, w_name, c0, n, name):
                sp.dma_start(buf[:, :, at:at + n],
                             one(w_name, l)[:, :, c0:c0 + n].rearrange("o (k p) n -> p (o k) n", p=P))\
                    .then_inc(S[name], 16)

            for l in range(DEPTH):
                if l > 0:
                    sp.wait_ge(S["tr_full"], nth(l, "tr_full", 0))
                for r0, name, pat in ((ROW_CW, "conv_w", "o w (t c) -> (o w t) c"), (ROW_CB, "conv_b", "o (t c) -> (o t) c"),
                                      (ROW_LG, "ln_g", "o (t c) -> (o t) c"), (ROW_LB, "ln_b", "o (t c) -> (o t) c"),
                                      (ROW_PS, "pool_scale", "o (t c) -> (o t) c"), (ROW_NG, "norm_g", "o (t c) -> (o t) c")):
                    src = one(name, l).rearrange(pat, c=P)
                    sp.dma_start(prow[r0:r0 + src.shape[0], :], src).then_inc(S["par_in"], 16)
                for r0, name in ((ROW_QN, "q_norm_g"), (ROW_KN, "k_norm_g")):
                    for h in range(2):
                        sp.dma_start(prow[r0:r0 + 1, h * HD:(h + 1) * HD], one(name, l)).then_inc(S["par_in"], 16)
                if l > 0:
                    sp.wait_ge(S["pj_full"], nth(l - 1, "pj_full", NPROJ))
                for name, c0, s in (("q", 0, "wq_q"), ("k", C_ATT, "wq_k"), ("v", 2 * C_ATT, "wq_v")):
                    weights(l, wq, c0, "w_in", COL[name], C_ATT, s)
                sp.dma_start(st_conv[:, :, :], one("state_conv", l).rearrange("o (r s) w c -> (o s w) r c", r=2)
                             ).then_inc(S["st_in"], 16)
                sp.dma_start(st_pool[:, :], one("state_pool", l).rearrange("o s w c -> (o s w) c")).then_inc(S["st_in"], 16)
                sp.wait_ge(zeroed, 1)
                if l > 0:
                    sp.wait_ge(S["rt_full"], nth(l, "rt_full", 0))
                for g in range(len(POOL_WINDOWS)):
                    r = 64 * (g % 2)
                    sp.dma_start(pw[r:r + 64, g // 2, r:r + 64], one("pool_w", l)[:, g].rearrange("o c d -> (o c) d"))\
                        .then_inc(S["pw_in"], 16)
                if l > 0:
                    sp.wait_ge(S["pj_full"], nth(l, "pj_full", 0))
                weights(l, wa, 0, "w_in", COL["a_val"], C_CONV, "wa_val")
                weights(l, wa, C_CONV, "w_in", COL["a_glu"], C_CONV, "wa_glu")
                sp.wait_ge(x_copied, XROUNDS)
                if l > 0:
                    sp.wait_ge(S["st_full"], nth(l, "st_full", 0))
                gather("k", l, "k_in")
                weights(l, wa, 2 * C_CONV, "w_in", COL["a_gate"], C_CONV, "wa_gate")
                for name, out, keep in (("state_conv", o_conv_s, TAIL - 1), ("state_pool", o_pool_s, POOL_BUF - 1)):
                    sp.dma_start(out[bass.ds(l, 1), :, 0:keep].rearrange("o s w c -> (o s) (w c)"),
                                 one(name, l)[:, :, 1:keep + 1].rearrange("o s w c -> (o s) (w c)"))\
                        .then_inc(S["state_out"], 16)
                bulk_pairs(l * PAIRS_IN, PAIRS_A)
                sp.wait_ge(S["pj_full"], nth(l, "pj_full", 9))
                weights(l, wq, 2 * C_POOL, "w_in", COL["c_gate"], C_ATT, "wq_c")
                weights(l, wq, 0, "w_in", COL["b_val"], 2 * C_POOL, "wq_b")
                bulk_pairs(l * PAIRS_IN + PAIRS_A, PAIRS_B)
                sp.wait_ge(S["ks_used"], nth(l, "ks_used", 1))
                gather("v", l, "v_in")
                sp.wait_ge(S["pj_full"], nth(l, "pj_full", PIDX[("a_gate", CT - 1)] + 1))
                for h in range(2):
                    weights(l, wa, h * 512, "w_out", h * 512, 512, f"wo_{h}")
                bulk_pairs(l * PAIRS_IN + PAIRS_A + PAIRS_B, PAIRS_C)
            bulk_pairs(DEPTH * PAIRS_IN, PAIRS - DEPTH * PAIRS_IN)
            sp.wait_ge(bulk_out, 16 * 2 * PAIRS)
            for name in ("v_out", "k_out", "new_out", "tail_out", "state_out"):
                sp.wait_ge(S[name], DEPTH * per[name])
            sp.wait_ge(y_out, 32)

        @block.gpsimd
        def _(pool):
            for name in (*START, *STAGED):
                pool.sem_inc(S[name], 1)
            for l in range(DEPTH - 1):
                for name, stored in STAGED.items():
                    pool.wait_ge(S[stored], nth(l, stored, per[stored]))
                    pool.sem_inc(S[name], 1)

        @block.tensor
        def _(pe):
            def turn(out, in_, rows):
                return nc.tensor.transpose(out, in_, C["ident"][0:rows, 0:rows])

            pe.wait_ge(const_in, 16)
            pe.wait_ge(x_in, 32)
            for u in range(XROUNDS):
                if u >= 2:
                    pe.wait_ge(x_copied, u - 1)
                out = (psc, po)[u % 2]
                if u < 4:
                    r, k0 = u // 2, 4 * (u % 2)
                    for k in range(4):
                        col = r * D_MODEL + (k0 + k) * P
                        last = turn(out[:, k * P:(k + 1) * P], x_tok[:, col:col + P], P)
                else:
                    for k in range(KD):
                        col = 2 * D_MODEL + k * P
                        last = turn(out[:, k * NS:(k + 1) * NS], x_tok[0:NS, col:col + P], NS)
                last.then_inc(x_turned, 1)

            with pe.Fori(0, DEPTH) as l:
                def tr_use(step):
                    pe.wait_ge(S["tr_free"], nth(l, "tr_free", TR[step]))

                for step in SCHEDULE:
                    kind = step[0] if isinstance(step, tuple) else step
                    if kind == "par":
                        pe.wait_ge(S["par_in"], nth(l, "par_in", per["par_in"]))
                        tr_use(step)
                        turn(ptr[:, 0:ROWS], prow[:, :], ROWS).then_inc(S["tr_full"], 1)
                    elif kind == "st0":
                        pe.wait_ge(S["st_in"], nth(l, "st_in", per["st_in"]))
                        tr_use(step)
                        for t in range(2):
                            for r in range(2):
                                c = (2 * t + r) * 120
                                last = turn(ptr[:, c:c + 120], st_conv[:, r, t * P:(t + 1) * P], 120)
                        last.then_inc(S["tr_full"], 1)
                    elif kind == "st1":
                        tr_use(step)
                        for r in range(2):
                            turn(ptr[:, r * 120:r * 120 + 120], st_conv[:, r, 2 * P:3 * P], 120)
                        for t in range(PT_):
                            last = turn(ptr[:, 240 + t * 120:360 + t * 120], st_pool[:, t * P:(t + 1) * P], 120)
                        last.then_inc(S["tr_full"], 1)
                    elif kind == "rms":
                        pe.wait_ge(S["st_free"], nth(l, "st_free", ST[step]))
                        pe.wait_ge(S["xsq"], nth(l, "xsq", 1))
                        for k in range(KD):
                            last = nc.tensor.matmul(ps[:, 0:T], C["ones"], mix[:, k, :], start=(k == 0), stop=(k == KD - 1))
                        last.then_inc(S["st_full"], 1)
                    elif kind == "proj":
                        n = step[1]
                        group, t, buf, col = PROJ[n]
                        if n == 0:
                            pe.wait_ge(S["h_ok"], nth(l, "h_ok", 1))
                        if t == 0:
                            pe.wait_ge(S[{"q": "wq_q", "k": "wq_k", "v": "wq_v", "a_val": "wa_val", "a_glu": "wa_glu",
                                         "a_gate": "wa_gate", "c_gate": "wq_c", "b_val": "wq_b", "b_gate": "wq_b"}[group]], nth(l, {"q": "wq_q", "k": "wq_k", "v": "wq_v", "a_val": "wa_val", "a_glu": "wa_glu",
                                         "a_gate": "wa_gate", "c_gate": "wq_c", "b_val": "wq_b", "b_gate": "wq_b"}[group], 16))
                        pe.wait_ge(S[f"pj_free{n % RING}"], nth(l, f"pj_free{n % RING}", n // RING))
                        for k in range(KD):
                            last = nc.tensor.matmul(pj[n % RING][:, 0:T], wbuf[buf][:, k, col:col + P], hT[:, k, :],
                                                    start=(k == 0), stop=(k == KD - 1))
                        last.then_inc(S["pj_full"], 1)
                    elif kind == "norm":
                        i = step[1]
                        pe.wait_ge(S["qk_raw"], nth(l, "qk_raw", i + 1))
                        pe.wait_ge(S["st_free"], nth(l, "st_free", ST[step]))
                        nc.tensor.matmul(ps[:, 0:T], C["heads"], sq[:, i % 2, :], start=True, stop=True).then_inc(S["st_full"], 1)
                        pe.wait_ge(S["rt_free"], nth(l, "rt_free", i))
                        nc.tensor.matmul(prt[:, 0:T], C["rot"], qg[:, i % 2, :], start=True, stop=True).then_inc(S["rt_full"], 1)
                    elif kind in ("vtok", "ktok"):
                        j = step[1]
                        if kind == "vtok":
                            pe.wait_ge(S["v_raw"], nth(l, "v_raw", AT))
                        else:
                            pe.wait_ge(S["qk_ok"], nth(l, "qk_ok", 2 * AT))
                        tr_use(step)
                        for t in range(AT):
                            src = vT[:, t, j * P:(j + 1) * P] if kind == "vtok" else qk[:, AT + t, j * P:(j + 1) * P]
                            last = turn(ptr[:, t * P:(t + 1) * P], src, P)
                        last.then_inc(S["tr_full"], 1)
                    elif kind in ("qb", "kb", "vb"):
                        i = ("qb", "kb", "vb").index(kind)
                        pe.wait_ge(S["rep_ok"], nth(l, "rep_ok", i + 1))
                        tr_use(step)
                        for t in range(AT):
                            last = turn(ptr[:, t * P:(t + 1) * P], rep[:, i, t, :], P)
                        last.then_inc(S["tr_full"], 1)
                    elif kind == "score":
                        h = step[1]
                        b = HD * (h % 2)
                        if h == 0:
                            pe.wait_ge(S["qk_ok"], nth(l, "qk_ok", 2 * AT))
                        pe.wait_ge(S["sc_free"], nth(l, "sc_free", h))
                        q, k = qk[b:b + HD, h // 2, :], qk[b:b + HD, AT + h // 2, :]
                        nc.tensor.matmul(psc[:, 0:P], q[:, 0:P], k[:, 0:P], start=True, stop=True)
                        nc.tensor.matmul(psc[:, P:3 * P], q[:, P:2 * P], k[:, 0:2 * P], start=True, stop=True)\
                            .then_inc(S["sc_full"], 1)
                    elif kind == "probT":
                        h = step[1]
                        pe.wait_ge(S["p_ok"], nth(l, "p_ok", h + 1))
                        tr_use(step)
                        for b in range(3):
                            last = turn(ptr[:, b * P:(b + 1) * P], sc[:, h % 2, b * P:(b + 1) * P], P)
                        last.then_inc(S["tr_full"], 1)
                    elif kind == "out":
                        h = step[1]
                        b = HD * (h % 2)
                        pe.wait_ge(S["tr_free"], nth(l, "tr_free", TR[("probT", h)] + 1))
                        if h % 2 == 0:
                            pe.wait_ge(S["o_free"], nth(l, "o_free", h // 2))
                        v0, v1 = (v_tok[:, j, h * HD:(h + 1) * HD] for j in range(2))
                        p_ = pT[:, h % 2, :]
                        nc.tensor.matmul(po[b:b + HD, 0:P], v0, p_[:, 0:P], start=True, stop=True)
                        nc.tensor.matmul(po[b:b + HD, P:2 * P], v0, p_[:, P:2 * P], start=True, stop=False)
                        nc.tensor.matmul(po[b:b + HD, P:2 * P], v1, p_[:, 2 * P:3 * P], start=False, stop=True)\
                            .then_inc(S["o_full"], 1)
                    elif kind == "spv":
                        pe.wait_ge(S["st_free"], nth(l, "st_free", ST[step]))
                        pe.wait_ge(S["spm_ok"], nth(l, "spm_ok", 1))
                        pe.wait_ge(S["tr_free"], nth(l, "tr_free", TR["vb"] + 1))
                        pe.wait_ge(S["v_in"], nth(l, "v_in", per["v_in"]))
                        for t in range(AT):
                            for j in range(SLOTS + 1):
                                v = kv[:, j, t * P:(t + 1) * P] if j < NEW else kvb[:, 1, t * P:(t + 1) * P]
                                w = spm[:, j * NH + 2 * t:j * NH + 2 * t + 2, :].rearrange("p h s -> p (h s)")
                                nc.tensor.matmul(ps[:, 2 * NS * t:2 * NS * (t + 1)], v, w, start=(j == 0), stop=(j == SLOTS))
                        nc.tensor.matmul(ps[:, 64:64 + NH * NS], C["ones"], spsum[:, :], start=True, stop=True)\
                            .then_inc(S["st_full"], 1)
                    elif kind == "poolw":
                        pe.wait_ge(S["pd_ok"], nth(l, "pd_ok", 1))
                        pe.wait_ge(S["pw_in"], nth(l, "pw_in", per["pw_in"]))
                        for t in range(PT_):
                            pe.wait_ge(S["rt_free"], nth(l, "rt_free", 2 * AT + t))
                            nc.tensor.matmul(prt[:, 0:T], pw[:, t, :], pd[:, t, :], start=True, stop=True)\
                                .then_inc(S["rt_full"], 1)
                    elif kind == "tails":
                        tr_use("conv_p")
                        for t in range(CT):
                            last = turn(ptr[0:TAIL, t * P:(t + 1) * P], u_ext[:, t, SEQ:SEQ + TAIL], P)
                        last.then_inc(S["tr_full"], 1)
                        tr_use("conv_s")
                        for t in range(CT):
                            last = turn(ptr[0:NS, t * P:(t + 1) * P], u_smp[:, t, :, TAIL], P)
                        last.then_inc(S["tr_full"], 1)
                        tr_use("pool_ps")
                        for t in range(PT_):
                            turn(ptr[0:POOL_BUF, t * P:(t + 1) * P], p_ext[:, t, SEQ:SEQ + POOL_BUF], P)
                            last = turn(ptr[0:NS, C_POOL + t * P:C_POOL + (t + 1) * P], p_smp[:, t, :, POOL_BUF], P)
                        last.then_inc(S["tr_full"], 1)
                    elif kind == "ln":
                        pe.wait_ge(S["conv_ok"], nth(l, "conv_ok", per["conv_ok"]))
                        pe.wait_ge(S["st_free"], nth(l, "st_free", ST["mean"]))
                        for t in range(CT):
                            last = nc.tensor.matmul(ps[:, 0:T], C["ones"], yc[:, t, :], start=(t == 0), stop=(t == CT - 1))
                        last.then_inc(S["st_full"], 1)
                        pe.wait_ge(S["ysq"], nth(l, "ysq", 1))
                        pe.wait_ge(S["st_free"], nth(l, "st_free", ST["var"]))
                        for t in range(CT):
                            last = nc.tensor.matmul(ps[:, 0:T], C["ones"], hT[:, t, :], start=(t == 0), stop=(t == CT - 1))
                        last.then_inc(S["st_full"], 1)
                    elif kind == "wout":
                        m = step[1]
                        n = NPROJ + m
                        if m == 0:
                            pe.wait_ge(S["mix_b"], nth(l, "mix_b", per["mix_b"]))
                            pe.wait_ge(S["mix_c"], nth(l, "mix_c", per["mix_c"]))
                            pe.wait_ge(S["mix_s"], nth(l, "mix_s", 1))
                            pe.wait_ge(S["mix_a"], nth(l, "mix_a", 1))
                        if m % 4 == 0:
                            pe.wait_ge(S[f"wo_{m // 4}"], nth(l, f"wo_{m // 4}", 16))
                        pe.wait_ge(S[f"pj_free{n % RING}"], nth(l, f"pj_free{n % RING}", n // RING))
                        for k in range(KD):
                            last = nc.tensor.matmul(pj[n % RING][:, 0:T], wa[:, k, m * P:(m + 1) * P], mix[:, k, :],
                                                    start=(k == 0), stop=(k == KD - 1))
                        last.then_inc(S["pj_full"], 1)

            pe.wait_ge(S["xT_ok"], nth(DEPTH - 1, "xT_ok", KD))
            for u in range(XROUNDS):
                if u >= 2:
                    pe.wait_ge(y_copied, u - 1)
                out = (psc, po)[u % 2]
                r, k0 = u // 2, 4 * (u % 2)
                if u < 4:
                    for k in range(4):
                        last = turn(out[:, k * P:(k + 1) * P], xT[:, k0 + k, r * P:(r + 1) * P], P)
                    last.then_inc(y_turned, 1)
                else:
                    for k in range(4):
                        turn(out[0:NS, k * P:(k + 1) * P], xT[:, k, SEQ:T], P)
                    for k in range(4):
                        last = turn(ptr[0:NS, k * P:(k + 1) * P], xT[:, 4 + k, SEQ:T], P)
                    last.then_inc(y_turned, 1)

        GATES = [(g, t) for g, t, _, _ in PROJ if g in ("a_glu", "c_gate", "a_gate", "b_gate")]
        GATE_SEM = {"a_glu": "u_ok", "c_gate": "sig_c_ok", "a_gate": "sig_a_ok", "b_gate": "sig_b_ok"}

        @block.scalar
        def _(act):
            A = nc.scalar.activation
            nc.scalar.preload_act_table_set("natural_log_exp_and_others")
            act.wait_ge(const_in, 16)
            with act.Fori(0, DEPTH) as l:
                def rsqrt_of(dst, src, scale, free_n, ok_sem, n):
                    A(dst, src, ACT.Ln, scale=scale, bias=C["eps"]).then_inc(S["st_free"], 1)
                    act.wait_ge(S["st_free"], nth(l, "st_free", free_n))
                    A(dst, dst, ACT.Exp, scale=-0.5).then_inc(S[ok_sem], 1)
                    act.wait_ge(S[ok_sem], nth(l, ok_sem, n))

                for step in SCHEDULE:
                    kind = step[0] if isinstance(step, tuple) else step
                    if kind == "st0":
                        act.wait_ge(S["tr_full"], nth(l, "tr_full", TR[step] + 1))
                        nc.scalar.copy(u_smp[:, 0:2, :, 0:TAIL],
                                            ptr[:, 0:480].rearrange("p (t s w) -> p t s w", t=2, s=NS)).then_inc(S["tr_free"], 1)
                        act.wait_ge(S["tr_free"], nth(l, "tr_free", TR[step] + 1))
                    elif kind == "st1":
                        act.wait_ge(S["tr_full"], nth(l, "tr_full", TR[step] + 1))
                        nc.scalar.copy(u_smp[:, 2, :, 0:TAIL], ptr[:, 0:240].rearrange("p (s w) -> p s w", s=NS))
                        nc.scalar.copy(p_smp[:, :, :, 0:POOL_BUF],
                                            ptr[:, 240:480].rearrange("p (t s w) -> p t s w", t=2, s=NS)).then_inc(S["tr_free"], 1)
                        act.wait_ge(S["tr_free"], nth(l, "tr_free", TR[step] + 1))
                    elif kind == "rms":
                        act.wait_ge(S["xT_ok"], nth(l, "xT_ok", 0))
                        A(mix[:, :, :], xT[:, :, :], ACT.Square).then_inc(S["xsq"], 1)
                        act.wait_ge(S["xsq"], nth(l, "xsq", 1))
                        act.wait_ge(S["st_full"], nth(l, "st_full", ST[step] + 1))
                        rsqrt_of(r_h[:, :], ps[:, 0:T], 1.0 / D_MODEL, ST[step] + 1, "r_h_ok", 1)
                    elif kind == "proj":
                        n = step[1]
                        group, t, _, _ = PROJ[n]
                        src = pj[n % RING][:, 0:T]
                        free = S[f"pj_free{n % RING}"]
                        act.wait_ge(S["pj_full"], nth(l, "pj_full", n + 1))
                        if group in "qk":
                            i = n
                            if i >= 2:
                                act.wait_ge(S["qk_ok"], nth(l, "qk_ok", i - 1))
                            A(sq[:, i % 2, :], src, ACT.Square)
                            gain = par[:, ROW_QN:ROW_QN + 1] if group == "q" else par[:, ROW_KN:ROW_KN + 1]
                            if i == 0:
                                act.wait_ge(S["tr_free"], nth(l, "tr_free", TR["par"] + 1))
                            A(qg[:, i % 2, :], src, ACT.Copy, scale=gain).then_inc(S["qk_raw"], 1)
                            act.wait_ge(S["qk_raw"], nth(l, "qk_raw", i + 1))
                            act.sem_inc(free, 1)
                        elif group == "v":
                            nc.scalar.copy(vT[:, t, :], src).then_inc(S["v_raw"], 1)
                            act.wait_ge(S["v_raw"], nth(l, "v_raw", t + 1))
                            act.sem_inc(free, 1)
                        elif group in ("a_glu", "c_gate", "a_gate", "b_gate"):
                            e = GATES.index((group, t))
                            if e >= 2:
                                group_b, t_b = GATES[e - 2]
                                act.wait_ge(S[GATE_SEM[group_b]], nth(l, GATE_SEM[group_b], t_b + 1))
                            A(ex[:, e % 2, :], src, ACT.Exp, scale=-1.0).then_inc(S["exp_ok"], 1)
                            act.wait_ge(S["exp_ok"], nth(l, "exp_ok", e + 1))
                        elif group == "b_val":
                            nc.scalar.copy(p_ext[:, t, POOL_BUF:], src[:, 0:SEQ])
                            nc.scalar.copy(p_smp[:, t, :, POOL_BUF], src[:, SEQ:T]).then_inc(S["b_val_ok"], 1)
                            act.wait_ge(S["b_val_ok"], nth(l, "b_val_ok", t + 1))
                            act.sem_inc(free, 1)
                    elif kind == "norm":
                        i = step[1]
                        act.wait_ge(S["st_full"], nth(l, "st_full", ST[step] + 1))
                        rsqrt_of(r_qk[:, i % 2, :], ps[:, 0:T], 1.0 / HD, ST[step] + 1, "qk_r", i + 1)
                    elif kind in ("vtok", "ktok"):
                        j = step[1]
                        tok, out, name = (v_tok, o_v_p, "v_out") if kind == "vtok" else (k_tok, o_k_p, "k_out")
                        if j == 0:
                            act.wait_ge(S[name[0] + "_staged"], nth(l, name[0] + "_staged", 0))
                        act.wait_ge(S["tr_full"], nth(l, "tr_full", TR[step] + 1))
                        nc.scalar.copy(tok[:, j, :], ptr[:, 0:C_ATT]).then_inc(S["tr_free"], 1)
                        act.wait_ge(S["tr_free"], nth(l, "tr_free", TR[step] + 1))
                        if j == 1:
                            act.dma_start(out[bass.ds(l, 1)].rearrange("l b (r p) h d -> p (l b r) (h d)", p=P),
                                          tok[:, :, :]).then_inc(S[name], 16)
                    elif kind == "rep":
                        act.wait_ge(S["qk_ok"], nth(l, "qk_ok", 2 * AT))
                        for i, src in enumerate((qk[:, 0:AT], qk[:, AT:2 * AT], vT[:, :])):
                            nc.scalar.copy(rep[:, i, :, :].rearrange("p t (s a) -> p t s a", s=NS),
                                                src[:, :, SEQ:T, None].to_broadcast([P, AT, NS, PER_S])).then_inc(S["rep_ok"], 1)
                            act.wait_ge(S["rep_ok"], nth(l, "rep_ok", i + 1))
                    elif kind in ("kb", "vb"):
                        j = 0 if kind == "kb" else 1
                        if kind == "kb":
                            act.wait_ge(S["new_staged"], nth(l, "new_staged", 0))
                        act.wait_ge(S["tr_full"], nth(l, "tr_full", TR[step] + 1))
                        nc.scalar.copy(kvb[:, j, :], ptr[:, 0:C_ATT]).then_inc(S["tr_free"], 1)
                        act.wait_ge(S["tr_free"], nth(l, "tr_free", TR[step] + 1))
                        out = (o_k_s, o_v_s)[j]
                        act.dma_start(out[bass.ds(l, 1), :, PAST - 1].rearrange("l s h d -> (l s) (h d)"),
                                      kvb[0:P:PER_S, j, :]).then_inc(S["new_out"], 16)
                    elif kind == "soft":
                        h = step[1]
                        act.wait_ge(S["nmax_ok"], nth(l, "nmax_ok", h + 1))
                        A(sc[:, h % 2, 0:P], sc[:, h % 2, 0:P], ACT.Exp, bias=nmax[:, h % 2, 0:1],
                          accum_out=lsum[:, h % 2, 0:1])
                        A(sc[:, h % 2, P:3 * P], sc[:, h % 2, P:3 * P], ACT.Exp, bias=nmax[:, h % 2, 1:2],
                               accum_out=lsum[:, h % 2, 1:2]).then_inc(S["p_raw"], 1)
                        act.wait_ge(S["p_raw"], nth(l, "p_raw", h + 1))
                    elif kind == "probT":
                        h = step[1]
                        if h >= 2:
                            act.wait_ge(S["o_full"], nth(l, "o_full", h - 1))
                        act.wait_ge(S["tr_full"], nth(l, "tr_full", TR[step] + 1))
                        nc.scalar.copy(pT[:, h % 2, :], ptr[:, 0:3 * P]).then_inc(S["tr_free"], 1)
                        act.wait_ge(S["tr_free"], nth(l, "tr_free", TR[step] + 1))
                    elif kind == "ssoft1":
                        act.wait_ge(S["ssub"], nth(l, "ssub", 1))
                        A(spr[:, :, :], ssc[:, :, :], ACT.Exp).then_inc(S["sexp"], 1)
                        act.wait_ge(S["sexp"], nth(l, "sexp", 1))
                    elif kind == "tails":
                        act.wait_ge(S["tail_staged"], nth(l, "tail_staged", 0))
                        for name, copies in (("conv_p", ((t_conv_p, ptr[0:TAIL, 0:C_CONV], o_conv_p, "l b w c -> (l b w) c", None),)),
                                             ("conv_s", ((t_conv_s, ptr[0:NS, 0:C_CONV], o_conv_s, None, TAIL - 1),)),
                                             ("pool_ps", ((t_pool_p, ptr[0:POOL_BUF, 0:C_POOL], o_pool_p, "l b w c -> (l b w) c", None),
                                                          (t_pool_s, ptr[0:NS, C_POOL:2 * C_POOL], o_pool_s, None, POOL_BUF - 1)))):
                            act.wait_ge(S["tr_full"], nth(l, "tr_full", TR[name] + 1))
                            for dst, src, _, _, _ in copies:
                                last = nc.scalar.copy(dst[:, :], src)
                            last.then_inc(S["tr_free"], 1)
                            act.wait_ge(S["tr_free"], nth(l, "tr_free", TR[name] + 1))
                            for dst, _, out, pat, row in copies:
                                o = out[bass.ds(l, 1)].rearrange(pat) if pat else \
                                    out[bass.ds(l, 1), :, row].rearrange("l s c -> (l s) c")
                                act.dma_start(o, dst[:, :]).then_inc(S["tail_out"], 16)
                    elif kind == "ln":
                        act.wait_ge(S["yc_ok"], nth(l, "yc_ok", 1))
                        act.wait_ge(S["pj_full"], nth(l, "pj_full", NPROJ))
                        A(hT[:, 0:CT, :], yc[:, :, :], ACT.Square).then_inc(S["ysq"], 1)
                        act.wait_ge(S["ysq"], nth(l, "ysq", 1))
                        act.wait_ge(S["st_full"], nth(l, "st_full", ST["var"] + 1))
                        rsqrt_of(r_h[:, :], ps[:, 0:T], 1.0 / C_CONV, ST["var"] + 1, "rstd_ok", 1)
                        act.wait_ge(S["z_ok"], nth(l, "z_ok", 1))
                        A(hT[:, CT:2 * CT, :], yc[:, :, :], ACT.Exp, scale=-1.0).then_inc(S["zexp"], 1)
                        act.wait_ge(S["zexp"], nth(l, "zexp", 1))

            for u in range(XROUNDS):
                act.wait_ge(y_turned, u + 1)
                src = (psc, po)[u % 2]
                r, k0 = u // 2, 4 * (u % 2)
                if u < 4:
                    nc.scalar.copy(x_tok[:, r * D_MODEL + k0 * P:r * D_MODEL + (k0 + 4) * P], src[:, :]).then_inc(y_copied, 1)
                else:
                    nc.scalar.copy(x_tok[0:NS, 2 * D_MODEL:2 * D_MODEL + 512], src[0:NS, :])
                    nc.scalar.copy(x_tok[0:NS, 2 * D_MODEL + 512:3 * D_MODEL], ptr[0:NS, :]).then_inc(y_copied, 1)
            act.wait_ge(y_copied, XROUNDS)
            act.dma_start(y_prompt.rearrange("b (r p) d -> p (b r) d", p=P),
                          x_tok[:, 0:2 * D_MODEL].rearrange("p (r d) -> p r d", r=2)).then_inc(y_out, 16)
            act.dma_start(y_sample.rearrange("s t d -> (s t) d"), x_tok[0:NS, 2 * D_MODEL:3 * D_MODEL]).then_inc(y_out, 16)

        @block.vector
        def _(dve):
            V = nc.vector
            V.memset(u_ext[:, :, 0:TAIL], 0.0)
            V.memset(p_ext[:, :, 0:POOL_BUF], 0.0)
            V.memset(mx[:, :, :], 0.0)
            V.memset(pw[:, :, :], 0.0).then_inc(zeroed, 1)
            dve.wait_ge(zeroed, 1)
            for u in range(XROUNDS):
                dve.wait_ge(x_turned, u + 1)
                src = (psc, po)[u % 2]
                if u < 4:
                    r, k0 = u // 2, 4 * (u % 2)
                    V.tensor_copy(xT[:, k0:k0 + 4, r * P:(r + 1) * P], src[:, :].rearrange("p (k c) -> p k c", k=4))\
                        .then_inc(x_copied, 1)
                else:
                    V.tensor_copy(xT[:, :, SEQ:T], src[:, 0:KD * NS].rearrange("p (k c) -> p k c", k=KD)).then_inc(x_copied, 1)
            dve.wait_ge(x_copied, XROUNDS)
            dve.sem_inc(S["xT_ok"], 1)

            with dve.Fori(0, DEPTH) as l:
                chain = [0]

                def link(ins):
                    chain[0] += 1
                    ins.then_inc(dve_done, 1)
                    dve.wait_ge(dve_done, l * DVE_LINKS + chain[0])

                def gate(group, t, n, dst_sem):
                    e = GATES.index((group, t))
                    dve.wait_ge(S["exp_ok"], nth(l, "exp_ok", e + 1))
                    link(V.tensor_scalar_add(ex[:, e % 2, :], ex[:, e % 2, :], 1.0))
                    link(V.reciprocal(ex[:, e % 2, :], ex[:, e % 2, :]))
                    return ex[:, e % 2, :]

                for step in SCHEDULE:
                    kind = step[0] if isinstance(step, tuple) else step
                    if kind == "par":
                        dve.wait_ge(S["tr_full"], nth(l, "tr_full", TR[step] + 1))
                        V.tensor_copy(par[:, :], ptr[:, 0:ROWS]).then_inc(S["tr_free"], 1)
                        dve.wait_ge(S["tr_free"], nth(l, "tr_free", TR[step] + 1))
                    elif kind == "rms":
                        dve.wait_ge(S["r_h_ok"], nth(l, "r_h_ok", 1))
                        for k in range(KD):
                            last = V.scalar_tensor_tensor(out=hT[:, k, :], in0=xT[:, k, :], scalar=par[:, ROW_NG + k:ROW_NG + k + 1],
                                                          in1=r_h[:, :], op0=ALU.mult, op1=ALU.mult)
                        last.then_inc(S["h_ok"], 1)
                        dve.wait_ge(S["h_ok"], nth(l, "h_ok", 1))
                    elif kind == "norm":
                        i = step[1]
                        dve.wait_ge(S["qk_raw"], nth(l, "qk_raw", i + 1))
                        V.tensor_tensor(roped[:, :], qg[:, i % 2, :], C["cos"], ALU.mult)
                        dve.wait_ge(S["rt_full"], nth(l, "rt_full", i + 1))
                        V.tensor_tensor(ropes[:, :], prt[:, 0:T], C["sin"], ALU.mult).then_inc(S["rt_free"], 1)
                        dve.wait_ge(S["rt_free"], nth(l, "rt_free", i + 1))
                        link(V.tensor_tensor(roped[:, :], roped[:, :], ropes[:, :], ALU.add))
                        dve.wait_ge(S["qk_r"], nth(l, "qk_r", i + 1))
                        V.tensor_tensor(qk[:, i, :], roped[:, :], r_qk[:, i % 2, :], ALU.mult).then_inc(S["qk_ok"], 1)
                        dve.wait_ge(S["qk_ok"], nth(l, "qk_ok", i + 1))
                    elif kind == "proj":
                        n = step[1]
                        group, t, _, _ = PROJ[n]
                        src = pj[n % RING][:, 0:T]
                        free = S[f"pj_free{n % RING}"]
                        if group == "a_glu":
                            s = gate(group, t, n, "u_ok")
                            dve.sem_inc(free, 1)
                            val = pj[(n - 1) % RING][:, 0:T]
                            V.tensor_tensor(u_ext[:, t, TAIL:], val[:, 0:SEQ], s[:, 0:SEQ], ALU.mult)
                            V.tensor_tensor(u_smp[:, t, :, TAIL], val[:, SEQ:T], s[:, SEQ:T], ALU.mult).then_inc(S["u_ok"], 1)
                            dve.wait_ge(S["u_ok"], nth(l, "u_ok", t + 1))
                            dve.sem_inc(S[f"pj_free{(n - 1) % RING}"], 1)
                        elif group in ("c_gate", "a_gate", "b_gate"):
                            dst, name = {"c_gate": (sig_c, "sig_c_ok"), "a_gate": (sig_a, "sig_a_ok"), "b_gate": (sig_b, "sig_b_ok")}[group]
                            s = gate(group, t, n, name)
                            V.tensor_tensor(dst[:, t, :], src, s, ALU.mult).then_inc(S[name], 1)
                            dve.wait_ge(S[name], nth(l, name, t + 1))
                            dve.sem_inc(free, 1)
                    elif kind == "qb":
                        dve.wait_ge(S["tr_full"], nth(l, "tr_full", TR[step] + 1))
                        V.tensor_copy(qb[:, :], ptr[:, 0:C_ATT]).then_inc(S["tr_free"], 1)
                        dve.wait_ge(S["tr_free"], nth(l, "tr_free", TR[step] + 1))
                    elif kind == "score":
                        h = step[1]
                        dve.wait_ge(S["sc_full"], nth(l, "sc_full", h + 1))
                        if h >= 2:
                            dve.wait_ge(S["tr_full"], nth(l, "tr_full", TR[("probT", h - 2)] + 1))
                        V.scalar_tensor_tensor(out=sc[:, h % 2, :], in0=psc[:, 0:3 * P], scalar=SCALE, in1=C["bias"],
                                                    op0=ALU.mult, op1=ALU.add).then_inc(S["sc_free"], 1)
                        dve.wait_ge(S["sc_free"], nth(l, "sc_free", h + 1))
                        V.tensor_reduce(nmax[:, h % 2, 0:1], sc[:, h % 2, 0:P], AX.X, ALU.max, negate=True)
                        V.tensor_reduce(nmax[:, h % 2, 1:2], sc[:, h % 2, P:3 * P], AX.X, ALU.max, negate=True).then_inc(S["nmax_ok"], 1)
                        dve.wait_ge(S["nmax_ok"], nth(l, "nmax_ok", h + 1))
                    elif kind == "probT":
                        h = step[1]
                        dve.wait_ge(S["p_raw"], nth(l, "p_raw", h + 1))
                        link(V.reciprocal(rl[:, h % 2, :], lsum[:, h % 2, :]))
                        V.tensor_scalar(sc[:, h % 2, 0:P], sc[:, h % 2, 0:P], rl[:, h % 2, 0:1], None, ALU.mult)
                        V.tensor_scalar(sc[:, h % 2, P:3 * P], sc[:, h % 2, P:3 * P], rl[:, h % 2, 1:2], None, ALU.mult).then_inc(S["p_ok"], 1)
                        dve.wait_ge(S["p_ok"], nth(l, "p_ok", h + 1))
                    elif kind == "out":
                        h = step[1]
                        if h % 2:
                            t = h // 2
                            dve.wait_ge(S["o_full"], nth(l, "o_full", h + 1))
                            dve.wait_ge(S["sig_c_ok"], nth(l, "sig_c_ok", t + 1))
                            V.tensor_tensor(mix[:, CT + PT_ + t, 0:SEQ], po[:, 0:SEQ], sig_c[:, t, 0:SEQ], ALU.mult).then_inc(S["mix_c"], 1)
                            dve.wait_ge(S["mix_c"], nth(l, "mix_c", t + 1))
                            dve.sem_inc(S["o_free"], 1)
                    elif kind == "sscore":
                        i = step[1]
                        a, b = SCORE_CUTS[i]
                        if i == 0:
                            dve.wait_ge(S["k_in"], nth(l, "k_in", per["k_in"]))
                            dve.wait_ge(S["tr_free"], nth(l, "tr_free", TR["kb"] + 1))
                            link(V.tensor_tensor(prod[:, :], kvb[:, 0, :], qb[:, :], ALU.mult))
                            V.tensor_reduce(ssc[:, NEW, :], prod[:, :].rearrange("p (h d) -> p h d", h=NH), AX.X, ALU.add)
                        link(V.tensor_tensor(kv[:, a:b, :], kv[:, a:b, :], qb[:, None, :].to_broadcast([P, b - a, C_ATT]), ALU.mult))
                        last = V.tensor_reduce(ssc[:, a:b, :], kv[:, a:b, :].rearrange("p j (h d) -> p j h d", h=NH), AX.X, ALU.add)
                        if i == len(SCORE_CUTS) - 1:
                            last.then_inc(S["ks_used"], 1)
                            dve.wait_ge(S["ks_used"], nth(l, "ks_used", 1))
                        else:
                            link(last)
                    elif kind == "ssoft0":
                        link(V.scalar_tensor_tensor(out=ssc[:, :, :], in0=ssc[:, :, :], scalar=SCALE,
                                                    in1=C["sbias"][:, :, None].to_broadcast([P, SLOTS + 1, NH]),
                                                    op0=ALU.mult, op1=ALU.add))
                        link(V.tensor_reduce(mx[:, 0, 0:NH], ssc[:, :, :].rearrange("p j h -> p h j"), AX.X, ALU.max))
                        link(V.transpose(mx[:, 1, :], mx[:, 0, :]))
                        link(V.tensor_reduce(mx2[:, :], mx[:, 1, :].rearrange("p (g a) -> p g a", g=2), AX.X, ALU.max))
                        link(V.tensor_copy(mx[:, 2, :].rearrange("p (g a) -> p g a", g=2), mx2[:, :, None].to_broadcast([P, 2, PER_S])))
                        link(V.transpose(mx[:, 3, :], mx[:, 2, :]))
                        V.tensor_tensor(ssc[:, :, :], ssc[:, :, :], mx[:, 3, None, 0:NH].to_broadcast([P, SLOTS + 1, NH]),
                                             ALU.subtract).then_inc(S["ssub"], 1)
                        dve.wait_ge(S["ssub"], nth(l, "ssub", 1))
                    elif kind == "ssoft1":
                        dve.wait_ge(S["sexp"], nth(l, "sexp", 1))
                        link(V.tensor_tensor(spm[:, :, :],
                                             spr[:, :, :].rearrange("p j h -> p (j h)")[:, :, None].to_broadcast([P, (SLOTS + 1) * NH, NS]),
                                             C["mask"][:, None, :].to_broadcast([P, (SLOTS + 1) * NH, NS]), ALU.mult))
                        V.tensor_reduce(spsum[:, :], spm[:, :, :].rearrange("p (j h) s -> p (h s) j", h=NH), AX.X, ALU.add).then_inc(S["spm_ok"], 1)
                        dve.wait_ge(S["spm_ok"], nth(l, "spm_ok", 1))
                    elif kind == "spv":
                        dve.wait_ge(S["st_full"], nth(l, "st_full", ST[step] + 1))
                        link(V.reciprocal(srl[:, :], ps[:, 64:64 + NH * NS]))
                        V.tensor_tensor(so[:, :, :, :].rearrange("p t e s -> p (t e s)"), ps[:, 0:NH * NS], srl[:, :], ALU.mult).then_inc(S["st_free"], 1)
                        dve.wait_ge(S["st_free"], nth(l, "st_free", ST[step] + 1))
                        for e in range(2):
                            b = HD * e
                            last = V.tensor_tensor(mix[b:b + HD, CT + PT_:KD, SEQ:T], so[b:b + HD, :, e, :], sig_c[b:b + HD, :, SEQ:T], ALU.mult)
                        last.then_inc(S["mix_s"], 1)
                        dve.wait_ge(S["mix_s"], nth(l, "mix_s", 1))
                    elif kind == "conv":
                        if step[1] == 0:
                            dve.wait_ge(S["u_ok"], nth(l, "u_ok", CT))
                        for c in range(step[1], step[2]):
                            w, t = divmod(c, CT)
                            x_w = u_ext[:, t, w:w + SEQ]
                            if w == 0:
                                last = V.tensor_scalar(yc[:, t, 0:SEQ], x_w, par[:, ROW_CW + t:ROW_CW + t + 1],
                                                       par[:, ROW_CB + t:ROW_CB + t + 1], ALU.mult, ALU.add)
                            else:
                                dve.wait_ge(S["conv_ok"], nth(l, "conv_ok", c - CT + 1))
                                last = V.scalar_tensor_tensor(out=yc[:, t, 0:SEQ], in0=x_w,
                                                              scalar=par[:, ROW_CW + w * CT + t:ROW_CW + w * CT + t + 1],
                                                              in1=yc[:, t, 0:SEQ], op0=ALU.mult, op1=ALU.add)
                            last.then_inc(S["conv_ok"], 1)
                    elif kind == "sconv":
                        for t in range(CT):
                            link(V.tensor_tensor(uw[:, :, :], u_smp[:, t, :, :], cw[:, t, None, :].to_broadcast([P, NS, CONV_W]), ALU.mult))
                            link(V.tensor_reduce(yc[:, t, SEQ:T], uw[:, :, :], AX.X, ALU.add))
                            link(V.tensor_scalar_add(yc[:, t, SEQ:T], yc[:, t, SEQ:T], par[:, ROW_CB + t:ROW_CB + t + 1]))
                    elif kind == "pool":
                        dve.wait_ge(S["b_val_ok"], nth(l, "b_val_ok", PT_))
                        L = POOL_BUF + SEQ
                        lo, hi = slice(0, 64), slice(64, P)
                        V.tensor_tensor(pd[lo, 0, 0:SEQ], p_ext[lo, 0, 15:L], p_ext[lo, 0, 14:L - 1], ALU.add)
                        link(V.tensor_tensor(pa[hi, 1:L], p_ext[hi, 0, 1:L], p_ext[hi, 0, 0:L - 1], ALU.add))
                        link(V.tensor_tensor(pd[hi, 0, 0:SEQ], pa[hi, 15:L], pa[hi, 13:L - 2], ALU.add))
                        link(V.tensor_tensor(pa[:, 1:L], p_ext[:, 1, 1:L], p_ext[:, 1, 0:L - 1], ALU.add))
                        link(V.tensor_tensor(pb[:, 3:L], pa[:, 3:L], pa[:, 1:L - 2], ALU.add))
                        V.tensor_tensor(pd[lo, 1, 0:SEQ], pb[lo, 15:L], pb[lo, 11:L - 4], ALU.add)
                        link(V.tensor_tensor(pa[hi, 7:L], pb[hi, 7:L], pb[hi, 3:L - 4], ALU.add))
                        V.tensor_tensor(pd[hi, 1, 0:SEQ], pa[hi, 15:L], pa[hi, 7:L - 8], ALU.add)
                        for g, w in enumerate(POOL_WINDOWS):
                            part = slice(64 * (g % 2), 64 * (g % 2) + 64)
                            last = V.tensor_reduce(pd[part, g // 2, SEQ:T], p_smp[part, g // 2, :, 16 - w:16], AX.X, ALU.add)
                        link(last)
                        link(V.tensor_tensor(pd[:, :, :], pd[:, :, :], C["inv_cnt"].rearrange("p (t c) -> p t c", t=PT_), ALU.mult))
                        V.tensor_tensor(pd[:, :, 0:SEQ], pd[:, :, 0:SEQ], p_ext[:, :, POOL_BUF:], ALU.subtract)
                        V.tensor_tensor(pd[:, :, SEQ:T], pd[:, :, SEQ:T], p_smp[:, :, :, POOL_BUF], ALU.subtract).then_inc(S["pd_ok"], 1)
                        dve.wait_ge(S["pd_ok"], nth(l, "pd_ok", 1))
                    elif kind == "poolw":
                        for t in range(PT_):
                            dve.wait_ge(S["rt_full"], nth(l, "rt_full", 2 * AT + t + 1))
                            dve.wait_ge(S["sig_b_ok"], nth(l, "sig_b_ok", t + 1))
                            V.scalar_tensor_tensor(out=mix[:, CT + t, :], in0=prt[:, 0:T], scalar=par[:, ROW_PS + t:ROW_PS + t + 1],
                                                        in1=sig_b[:, t, :], op0=ALU.mult, op1=ALU.mult).then_inc(S["mix_b"], 1)
                            dve.wait_ge(S["mix_b"], nth(l, "mix_b", t + 1))
                            dve.sem_inc(S["rt_free"], 1)
                    elif kind == "ln":
                        dve.wait_ge(S["st_full"], nth(l, "st_full", ST["mean"] + 1))
                        dve.wait_ge(S["conv_ok"], nth(l, "conv_ok", per["conv_ok"]))
                        V.scalar_tensor_tensor(out=yc[:, :, :], in0=ps[:, None, 0:T].to_broadcast([P, CT, T]), scalar=-1.0 / C_CONV,
                                               in1=yc[:, :, :], op0=ALU.mult, op1=ALU.add).then_inc(S["yc_ok"], 1)
                        dve.wait_ge(S["yc_ok"], nth(l, "yc_ok", 1))
                        dve.sem_inc(S["st_free"], 1)
                        dve.wait_ge(S["rstd_ok"], nth(l, "rstd_ok", 1))
                        link(V.tensor_tensor(yc[:, :, :], yc[:, :, :], r_h[:, None, :].to_broadcast([P, CT, T]), ALU.mult))
                        for t in range(CT):
                            last = V.tensor_scalar(yc[:, t, :], yc[:, t, :], par[:, ROW_LG + t:ROW_LG + t + 1],
                                                   par[:, ROW_LB + t:ROW_LB + t + 1], ALU.mult, ALU.add)
                        last.then_inc(S["z_ok"], 1)
                        dve.wait_ge(S["z_ok"], nth(l, "z_ok", 1))
                        link(V.tensor_tensor(sig_a[:, :, :], sig_a[:, :, :], yc[:, :, :], ALU.mult))
                        dve.wait_ge(S["zexp"], nth(l, "zexp", 1))
                        z = hT[:, CT:2 * CT, :]
                        link(V.tensor_scalar_add(z, z, 1.0))
                        link(V.reciprocal(z, z))
                        V.tensor_tensor(mix[:, 0:CT, :], sig_a[:, :, :], z, ALU.mult).then_inc(S["mix_a"], 1)
                        dve.wait_ge(S["mix_a"], nth(l, "mix_a", 1))
                    elif kind == "wout":
                        m = step[1]
                        n = NPROJ + m
                        dve.wait_ge(S["pj_full"], nth(l, "pj_full", n + 1))
                        V.tensor_tensor(xT[:, m, :], xT[:, m, :], pj[n % RING][:, 0:T], ALU.add).then_inc(S["xT_ok"], 1)
                        dve.wait_ge(S["xT_ok"], nth(l, "xT_ok", m + 1))
                        dve.sem_inc(S[f"pj_free{n % RING}"], 1)
                assert chain[0] == DVE_LINKS, chain[0]


DVE_LINKS = 68

_INS = ["x_prompt", "x_sample", "state_conv", "state_pool", "cache_k_win", "cache_v_win", "norm_g", "w_in", "conv_w",
        "conv_b", "ln_g", "ln_b", "pool_w", "pool_scale", "q_norm_g", "k_norm_g", "w_out"]
_OUTS = [(1, SEQ, D_MODEL), (NS, 1, D_MODEL), (DEPTH, 1, TAIL, C_CONV), (DEPTH, 1, POOL_BUF, C_POOL),
         (DEPTH, 1, SEQ, NH, HD), (DEPTH, 1, SEQ, NH, HD), (DEPTH, NS, TAIL, C_CONV), (DEPTH, NS, POOL_BUF, C_POOL),
         (DEPTH, NS, PAST, NH, HD), (DEPTH, NS, PAST, NH, HD)]


def kernel(**inputs):
    import concourse.bacc as bacc
    from concourse.bass_utils import run_bass_kernel_spmd as run

    nc = bacc.Bacc("TRN2", target_bir_lowering=False, num_devices=1, dynamic_dma_scratch_size=1024)
    arrays, ins = {}, {}
    for name in _INS:
        a = np.ascontiguousarray(inputs[name])
        arrays[f"in_{name}"] = a
        ins[name] = nc.dram_tensor(f"in_{name}", a.shape, F32, kind="ExternalInput").ap()
    at, table = constants()
    arrays["in_const"] = table
    const = nc.dram_tensor("in_const", table.shape, F32, kind="ExternalInput").ap()
    outs = [nc.dram_tensor(f"out_{i}", s, F32, kind="ExternalOutput").ap() for i, s in enumerate(_OUTS)]
    trunk_program(nc, ins, const, at, outs)
    r = run(nc, [arrays], core_ids=[0])
    return tuple(r.results[0][f"out_{i}"] for i in range(len(_OUTS)))
```

```python
from contextlib import ExitStack

import numpy as np

import concourse.bass as bass
from concourse import mybir

F32 = mybir.dt.float32
ALU = mybir.AluOpType
ACT = mybir.ActivationFunctionType
AX = mybir.AxisListType

P = 128
DEPTH, D_MODEL, SEQ, NS, PAST = 2, 1024, 256, 8, 2048
C_CONV, C_POOL, C_ATT, HD = 384, 256, 384, 64
NH = C_ATT // HD
CONV_W, POOL_BUF, POOL_WINDOWS = 31, 15, (2, 4, 8, 16)
DILATIONS, KEYS = (1, 4, 16), 128
EPS = 1e-6
D_IN = 3 * C_CONV + 2 * C_POOL + 4 * C_ATT
T = SEQ + NS
KD = D_MODEL // P
CT, PT_, AT = C_CONV // P, C_POOL // P, C_ATT // P
TAIL = CONV_W - 1
PER_S = P // NS
SCALE = float(HD) ** -0.5
MASKED = -1e30

GATHER = []
_hi = PAST
for _d in DILATIONS:
    _lo = PAST - _d * KEYS
    GATHER.append((_lo, _d, (_hi - _lo) // _d // PER_S))
    _hi = _lo
SLOTS = sum(g[2] for g in GATHER)
NEW = SLOTS
SCORE_CUTS = [(a, a + 4) for a in range(0, SLOTS, 4)]

COL = {}
_c = 0
for _n, _w in (("a_val", C_CONV), ("a_glu", C_CONV), ("a_gate", C_CONV), ("b_val", C_POOL), ("b_gate", C_POOL),
               ("q", C_ATT), ("k", C_ATT), ("v", C_ATT), ("c_gate", C_ATT)):
    COL[_n] = _c
    _c += _w

ROW_CW = 0
ROW_CB = CONV_W * CT
ROW_LG = ROW_CB + CT
ROW_LB = ROW_LG + CT
ROW_PS = ROW_LB + CT
ROW_NG = ROW_PS + PT_
ROW_QN = ROW_NG + KD
ROW_KN = ROW_QN + 1
ROWS = ROW_KN + 1

PROJ = []
for _t in range(CT):
    PROJ += [("a_val", _t, "w0", _t * P), ("a_glu", _t, "w0", C_CONV + _t * P)]
PROJ += [("a_gate", t, "w0", 2 * C_CONV + t * P) for t in range(CT)]
PROJ += [("q", t, "w1", t * P) for t in range(AT)]
PROJ += [("k", t, "w1", C_ATT + t * P) for t in range(AT)]
PROJ += [("v", t, "w1", 2 * C_ATT + t * P) for t in range(AT)]
PROJ += [("c_gate", t, "w0", 2 * C_POOL + t * P) for t in range(AT)]
PROJ += [("b_val", t, "w0", t * P) for t in range(PT_)]
PROJ += [("b_gate", t, "w0", C_POOL + t * P) for t in range(PT_)]
NPROJ = len(PROJ)
PIDX = {(g, t): n for n, (g, t, _, _) in enumerate(PROJ)}
GATES = [(g, t) for g, t, _, _ in PROJ if g in ("a_glu", "a_gate", "c_gate", "b_gate")]
GATE_USED = {"a_glu": "u_ok", "c_gate": "sig_c_ok", "a_gate": "sig_a_ok", "b_gate": "sig_b_ok"}
NGATES = len(GATES)
LIMIT = 2.0 ** 62
RING = 3
NRING = NPROJ + KD
assert NRING % RING == 0

CONV_TAPS = CONV_W * CT
_taps = {2: (5, 0, 0), 3: (5, 0, 0), 4: (4, 3, 0), 5: (4, 3, 0), 6: (2, 3, 3), 7: (2, 3, 3), 8: (1, 1, 1), 9: (2, 3, 3),
         10: (0, 2, 2), 11: (1, 1, 2), 12: (1, 1, 2), 13: (1, 1, 1), 14: (0, 1, 2), 15: (1, 1, 1), 16: (0, 1, 1), 17: (1, 1, 1),
         18: (0, 1, 2), 19: (1, 1, 2), 20: (0, 2, 2), 21: (0, 2, 3)}
SV_CUTS = [(0, 8), (8, 16), (16, SLOTS + 1)]
_behind = {
    1: ["st0"], 2: ["st1"], 8: ["sconv"],
    10: [("norm", 0), "conv_p"], 11: [("norm", 1), "conv_s"], 12: [("norm", 2), "rep_q"], 13: [("norm", 3), "qb", ("sscore", 0)],
    14: [("norm", 4), ("sscore", 1)], 15: [("norm", 5), ("sscore", 2)],
    16: [("score", 0), "rep_k", ("sscore", 3), ("pnorm", 0)],
    17: [("probT", 0), ("score", 1), "kb", ("sscore", 4), ("pnorm", 1), "rep_v"],
    18: [("probT", 1), ("score", 2), ("vtok", 0), ("vtok", 1), ("pnorm", 2), "snew", ("out", 0)],
    19: [("probT", 2), ("score", 3), ("out", 1), "vb", ("pnorm", 3), "ssoft0"],
    20: [("probT", 3), ("score", 4), ("out", 2), ("ktok", 0), ("pnorm", 4), "ssoft1"],
    21: [("probT", 4), ("score", 5), ("out", 3), ("ktok", 1), ("pnorm", 5)],
    22: [("probT", 5), "ln1", ("out", 4), ("out", 5), ("spv", 0), "pool"],
    23: ["ln2", "pool_ps", ("spv", 1), "ln3"],
    24: [("spv", 2), ("poolw", 0), ("poolw", 1), "spT"],
}


def taps_of(counts, done):
    left, out = list(counts), []
    while sum(left):
        t = max(range(CT), key=lambda i: (left[i] > 0, not (out and out[-1][1] == i), left[i]))
        out.append((done[t], t))
        done[t] += 1
        left[t] -= 1
    return out


SCHEDULE = ["par", "rms"]
TAPS = []
_done = [0] * CT
for _n in range(NPROJ):
    SCHEDULE.append(("proj", _n))
    _steps = list(_behind.get(_n, []))
    if PROJ[_n][0] in ("a_glu", "a_gate", "c_gate", "b_gate"):
        _at = [i for i, _s in enumerate(_steps) if _s[0] == "score"]
        _steps.insert(_at[0] + 1 if _at else 0, ("gate", _n))
    SCHEDULE += _steps
    if _n in _taps:
        _new = taps_of(_taps[_n], _done)
        SCHEDULE.append(("conv", len(TAPS), len(TAPS) + len(_new)))
        TAPS += _new
assert _done == [CONV_W] * CT, _done
SCHEDULE += [("wout", m) for m in range(KD)]

TR = {}
for _s in SCHEDULE:
    if _s in ("par", "st0", "st1", "qb", "kb", "vb", "conv_p", "conv_s", "pool_ps", "spT") or \
            (isinstance(_s, tuple) and _s[0] in ("vtok", "ktok", "probT")):
        TR[_s] = len(TR)
NTR = len(TR)
ST = {}
for _s in SCHEDULE:
    if _s in ("rms", "ln1", "ln2") or (isinstance(_s, tuple) and _s[0] == "norm"):
        ST[_s] = len(ST)
NST = len(ST)
NRT = 2 * AT + PT_

COPIES = 2 * DEPTH * NS
COPIES_AFTER = [{"a": 0, "keys": 2, "gates": 5, "values": 7},
                {"a": 2, "keys": 2, "gates": 4, "values": 10}]
assert sum(n for c in COPIES_AFTER for n in c.values()) == COPIES
XROUNDS = 5


def multiplicity(off):
    return sum((off >= 0) & (off % d == 0) & (off <= d * KEYS) for d in DILATIONS)


def constants():
    f = np.float32
    half = HD // 2
    inv = np.power(f(10000.0), -np.arange(half, dtype=f) / f(half)).astype(f)
    pos = np.concatenate([np.arange(SEQ), np.full(NS, PAST)]).astype(f)
    ang = (pos[None, :] * inv[:, None]).astype(f)
    part = np.arange(P)
    cos, sin = np.cos(ang)[part % half].astype(f), np.sin(ang)[part % half].astype(f)
    ident = np.eye(P, dtype=f)
    heads = (part[:, None] // HD == part[None, :] // HD).astype(f)
    rot = np.zeros((P, P), f)
    for m in range(P):
        rot[m + half if m % HD < half else m - half, m] = -1.0 if m % HD < half else 1.0

    def log_of(c):
        return np.where(c > 0, np.log(np.maximum(c, 1)), MASKED).astype(f)

    i, j = part[:, None], np.arange(SEQ)[None, :]
    bias = np.concatenate([log_of(multiplicity(i - j[:, :P])), log_of(multiplicity(P + i - j))], axis=1)
    a = part[:, None] % PER_S
    offs = [PAST - (lo + d * (n * a + np.arange(n)[None, :])) for lo, d, n in GATHER]
    sbias = np.concatenate([log_of(multiplicity(o)) for o in offs]
                           + [log_of(np.where(a == 0, multiplicity(np.zeros_like(a)), 0))], axis=1)
    mask = (part[:, None] // PER_S == np.arange(NS)[None, :]).astype(f)
    win = np.array(POOL_WINDOWS)[np.stack([part // 64, 2 + part // 64], axis=1)]
    first = np.minimum(np.arange(POOL_BUF + 1)[None, None, :] + 1, win[:, :, None])
    inv_cnt = (f(1.0) / first.astype(f)).astype(f).reshape(P, -1)
    inv_win = (f(1.0) / win.astype(f)).astype(f)
    eps = np.full((P, 1), EPS, f)
    parts = dict(ident=ident, eps=eps, heads=heads, rot=rot, cos=cos, sin=sin, bias=bias,
                 sbias=sbias, mask=mask, inv_cnt=inv_cnt, inv_win=inv_win)
    at, n = {}, 0
    for name, v in parts.items():
        at[name] = (n, n + v.shape[1])
        n += v.shape[1]
    return at, np.ascontiguousarray(np.concatenate(list(parts.values()), axis=1))


def trunk_program(nc, ins, const, const_at, outs):
    (y_prompt, y_sample, o_conv_p, o_pool_p, o_k_p, o_v_p, o_conv_s, o_pool_s, o_k_s, o_v_s) = outs
    with ExitStack() as ctx:
        def sb(name, shape):
            return ctx.enter_context(nc.sbuf_tensor(name, shape, F32))

        def bank(name):
            return ctx.enter_context(nc.psum_tensor(name, [P, 512], F32))

        def sem(name):
            return ctx.enter_context(nc.semaphore(name))

        cst = sb("cst", [P, const.shape[1]])
        C = {name: cst[:, a:b] for name, (a, b) in const_at.items()}
        ones = sb("ones", [P, P])
        w0 = sb("w0", [P, KD, 3 * C_CONV])
        w1 = sb("w1", [P, KD, 3 * C_ATT])
        wbuf = {"w0": w0, "w1": w1}
        kv = sb("kv", [P, SLOTS, C_ATT])
        x_tok = kv[:, :, :].rearrange("p a b -> p (a b)")
        xT = sb("xT", [P, KD, T])
        hT = sb("hT", [P, KD, T])
        mix = sb("mix", [P, KD, T])
        prow = sb("prow", [ROWS, P])
        par = sb("par", [P, ROWS])
        cw = par[:, ROW_CW:ROW_CB].rearrange("p (w t) -> p t w", t=CT)
        qk = sb("qk", [P, 2 * AT, T])
        x_sum = sb("x_sum", [P, 3])
        diagonal = qk[:, 0, :]
        r_h = sb("r_h", [P, T])
        sqg = sb("sqg", [P, 4, T])
        sq, qg = sqg[:, 0:2, :], sqg[:, 2:4, :]
        lns = sqg[:, 0:CT, :]
        r_qk = sb("r_qk", [P, 2, T])
        roped = sb("roped", [P, T])
        ropes = sb("ropes", [P, T])
        vT = sb("vT", [P, AT, T])
        v_tok = sb("v_tok", [P, 2, C_ATT])
        k_tok = sb("k_tok", [P, 2, C_ATT])
        qb = sb("qb", [P, C_ATT])
        kvb = sb("kvb", [P, 2, C_ATT])
        rep = sb("rep", [P, AT, P])
        prod = sb("prod", [P, C_ATT])
        ssc = sb("ssc", [P, SLOTS + 1, NH])
        spr = sb("spr", [P, SLOTS + 1, NH])
        spm = sb("spm", [P, (SLOTS + 1) * NH, NS])
        spsum = sb("spsum", [P, NH * NS])
        srl = sb("srl", [NH * NS, 1])
        so = sb("so", [P, C_ATT])
        mx = sb("mx", [P, 4, 32])
        mx2 = sb("mx2", [P, 2])
        u_ext = sb("u_ext", [P, CT, TAIL + SEQ])
        u_smp = sb("u_smp", [P, CT, NS, CONV_W])
        uw = sb("uw", [P, NS, CONV_W])
        yc = sb("yc", [P, CT, T])
        sig_a = sb("sig_a", [P, CT, T])
        sig_b = sb("sig_b", [P, PT_, T])
        sig_c = sb("sig_c", [P, AT, T])
        ex = sb("ex", [P, 2, T])
        p_ext = sb("p_ext", [P, PT_, POOL_BUF + SEQ])
        p_smp = sb("p_smp", [P, PT_, NS, POOL_BUF + 1])
        pa = sb("pa", [P, POOL_BUF + SEQ])
        pb = sb("pb", [P, POOL_BUF + SEQ])
        pd = sb("pd", [P, PT_, T])
        pw = sb("pw", [P, PT_, P])
        sc = sb("sc", [P, 2, 3 * P])
        nmax = sb("nmax", [P, 2, 2])
        lsum = sb("lsum", [P, 2, 2])
        rl = sb("rl", [P, 2, 2])
        pT = sb("pT", [P, 2, 3 * P])
        st_conv = sb("st_conv", [NS * TAIL // 2, 2, C_CONV])
        st_pool = sb("st_pool", [NS * POOL_BUF, C_POOL])
        t_conv_p = sb("t_conv_p", [TAIL, C_CONV])
        t_conv_s = sb("t_conv_s", [NS, C_CONV])
        t_pool_p = sb("t_pool_p", [POOL_BUF, C_POOL])
        t_pool_s = sb("t_pool_s", [NS, C_POOL])

        pj = [bank(f"pj{i}") for i in range(RING)]
        ps = bank("ps")
        prt = bank("prt")
        psc = bank("psc")
        ptr = bank("ptr")
        po = bank("po")

        per = {}

        S = {}
        for name, n in dict(
                par_in=10 * 16, st_in=2 * 16, pw_in=4 * 16, q_in=16, k_w_in=16, v_w_in=16, b_in=16, c_in=16,
                a_val_in=16, a_glu_in=16, a_gate_in=16, wo_0=16, wo_1=16, k_in=3 * NS * 16, v_in=3 * NS * 16,
                v_out=16, k_out=16, new_out=2 * 16, tail_out=4 * 16, state_out=2 * 16,
                pj_full=NRING, pj_free0=NRING // RING, pj_free1=NRING // RING, pj_free2=NRING // RING,
                tr_full=NTR, tr_free=NTR, st_full=NST, st_free=NST, rt_full=NRT, rt_free=NRT,
                sc_full=NH + 1, sc_free=NH + 1, o_full=NH, o_free=AT,
                xsq=KD, r_h_ok=1, h_ok=KD, qk_raw=2 * AT, qk_r=2 * AT, qk_ok=2 * AT,
                v_raw=AT, rep_ok=3, exp_ok=NGATES, clamp_ok=NGATES, sig_ok=NGATES, u_ok=CT, sig_c_ok=AT, sig_a_ok=CT, sig_b_ok=PT_,
                nmax_ok=NH, p_raw=NH, p_ok=NH, kprod_ok=len(SCORE_CUTS), ks_used=1, ssub=1, sexp=1, spm_ok=1, so_ok=1,
                conv_ok=CONV_TAPS, yc_ok=1,
                ysq=1, rstd_ok=1, z_ok=1, zexp=1, zclamp=1, zsig=1, b_val_ok=PT_, pd_ok=1,
                mix_a=1, mix_b=PT_, mix_c=AT, mix_s=1, xT_ok=KD).items():
            S[name] = sem(name)
            per[name] = n
        early_in, const_in, x_in = sem("early_in"), sem("const_in"), sem("x_in")
        squared, diagonal_ok = sem("squared"), sem("diagonal_ok")
        bulk_out, y_out = sem("bulk_out"), sem("y_out")
        zeroed, x_turned, x_copied = sem("zeroed"), sem("x_turned"), sem("x_copied")
        y_turned, y_copied = sem("y_turned"), sem("y_copied")
        dve_done, act_done = sem("dve_done"), sem("act_done")

        block = ctx.enter_context(nc.Block())

        START = ("pj_free0", "pj_free1", "pj_free2", "tr_free", "rt_free", "sc_free", "o_free")
        STAGED = {"v_staged": "v_out", "k_staged": "k_out", "new_staged": "new_out", "tail_staged": "tail_out"}
        for name in STAGED:
            S[name] = sem(name)
            per[name] = 1
        first = {name: 1 for name in (*START, *STAGED)}

        def nth(l, name, n):
            return l * per[name] + n + first.get(name, 0)

        cache = {"k": ins["cache_k_win"], "v": ins["cache_v_win"]}

        @block.sync
        def _(sp):
            copied = [0]
            chunk = (PAST - 1) // 16 * C_ATT

            def bulk(count):
                for kind, out, begin in (("k", o_k_s, 0), ("v", o_v_s, COPIES // 2)):
                    a = max(copied[0], begin) - begin
                    b = min(copied[0] + count - begin, COPIES // 2)
                    if a < b:
                        with sp.Fori(a, b) as i:
                            src = cache[kind].rearrange("l s t h d -> (l s) (t h d)")[bass.ds(i, 1)]
                            dst = out.rearrange("l s t h d -> (l s) (t h d)")[bass.ds(i, 1)]
                            sp.dma_start(dst[:, 0:16 * chunk].rearrange("o (c e f) -> (o c) e f", c=16, e=6),
                                         src[:, C_ATT:C_ATT + 16 * chunk].rearrange("o (c e f) -> (o c) e f", c=16, e=6))\
                                .then_inc(bulk_out, 16)
                copied[0] += count

            def bulk_rest():
                for kind, out in (("k", o_k_s), ("v", o_v_s)):
                    src = cache[kind].rearrange("l s t h d -> (l s) (t h d)")
                    dst = out.rearrange("l s t h d -> (l s) (t h d)")
                    sp.dma_start(dst[:, 16 * chunk:(PAST - 1) * C_ATT], src[:, C_ATT + 16 * chunk:]).then_inc(bulk_out, 16)

            def one(name, l):
                return ins[name][bass.ds(l, 1)]

            def gather(kind, l, name):
                at = 0
                for lo, d, n in GATHER:
                    for s in range(NS):
                        rows = one(f"cache_{kind}_win", l)[:, s, lo:lo + d * n * PER_S]
                        rows = rows.rearrange("o (a b e) h d -> (o a) b e (h d)", a=PER_S, e=d)[:, :, 0, :]
                        sp.dma_start(kv[s * PER_S:(s + 1) * PER_S, at:at + n, :], rows).then_inc(S[name], 16)
                    at += n

            def weights(l, buf, at, w_name, c0, n, name):
                sp.dma_start(buf[:, :, at:at + n],
                             one(w_name, l)[:, :, c0:c0 + n].rearrange("o (k p) n -> p (o k) n", p=P))\
                    .then_inc(S[name], 16)

            def params(l):
                if l > 0:
                    sp.wait_ge(S["tr_full"], nth(l - 1, "tr_full", TR["par"] + 1))
                for r0, name, pat in ((ROW_CW, "conv_w", "o w (t c) -> (o w t) c"), (ROW_CB, "conv_b", "o (t c) -> (o t) c"),
                                      (ROW_LG, "ln_g", "o (t c) -> (o t) c"), (ROW_LB, "ln_b", "o (t c) -> (o t) c"),
                                      (ROW_PS, "pool_scale", "o (t c) -> (o t) c"), (ROW_NG, "norm_g", "o (t c) -> (o t) c")):
                    src = one(name, l).rearrange(pat, c=P)
                    sp.dma_start(prow[r0:r0 + src.shape[0], :], src).then_inc(S["par_in"], 16)
                for r0, name in ((ROW_QN, "q_norm_g"), (ROW_KN, "k_norm_g")):
                    for h in range(2):
                        sp.dma_start(prow[r0:r0 + 1, h * HD:(h + 1) * HD], one(name, l)).then_inc(S["par_in"], 16)

            def states(l):
                if l > 0:
                    sp.wait_ge(S["tr_full"], nth(l - 1, "tr_full", TR["st1"] + 1))
                sp.dma_start(st_conv[:, :, :], one("state_conv", l).rearrange("o (r s) w c -> (o s w) r c", r=2)
                             ).then_inc(S["st_in"], 16)
                sp.dma_start(st_pool[:, :], one("state_pool", l).rearrange("o s w c -> (o s w) c")).then_inc(S["st_in"], 16)

            early = const_at["eps"][1]
            sp.dma_start(x_tok[:, 0:2 * D_MODEL].rearrange("p (r d) -> p r d", r=2),
                         ins["x_prompt"].rearrange("b (r p) d -> p (b r) d", p=P)).then_inc(x_in, 16)
            sp.dma_start(x_tok[0:NS, 2 * D_MODEL:3 * D_MODEL],
                         ins["x_sample"].rearrange("s t d -> (s t) d")).then_inc(x_in, 16)
            sp.dma_start(cst[:, 0:early], const[:, 0:early]).then_inc(early_in, 16)
            weights(0, w0, 0, "w_in", COL["a_val"], C_CONV, "a_val_in")
            params(0)
            weights(0, w0, C_CONV, "w_in", COL["a_glu"], C_CONV, "a_glu_in")
            sp.dma_start(cst[:, early:], const[:, early:]).then_inc(const_in, 16)
            for l in range(DEPTH):
                if l > 0:
                    sp.wait_ge(S["pj_full"], nth(l - 1, "pj_full", NPROJ))
                for name, c0 in (("a_val", 0), ("a_glu", C_CONV), ("a_gate", 2 * C_CONV)):
                    if l > 0 or name == "a_gate":
                        weights(l, w0, c0, "w_in", COL[name], C_CONV, f"{name}_in")
                if l == 0:
                    states(l)
                bulk(COPIES_AFTER[l]["a"])
                if l > 0:
                    sp.wait_ge(S["pj_full"], nth(l, "pj_full", 0))
                for name, c0, s in (("q", 0, "q_in"), ("k", C_ATT, "k_w_in"), ("v", 2 * C_ATT, "v_w_in")):
                    weights(l, w1, c0, "w_in", COL[name], C_ATT, s)
                sp.wait_ge(zeroed, 1)
                if l > 0:
                    sp.wait_ge(S["rt_full"], nth(l, "rt_full", 0))
                for g in range(len(POOL_WINDOWS)):
                    r = 64 * (g % 2)
                    sp.dma_start(pw[r:r + 64, g // 2, r:r + 64], one("pool_w", l)[:, g].rearrange("o c d -> (o c) d"))\
                        .then_inc(S["pw_in"], 16)
                sp.wait_ge(x_copied, XROUNDS)
                if l > 0:
                    sp.wait_ge(S["sc_full"], nth(l - 1, "sc_full", NH + 1))
                gather("k", l, "k_in")
                bulk(COPIES_AFTER[l]["keys"])
                sp.wait_ge(S["pj_full"], nth(l, "pj_full", PIDX[("a_gate", CT - 1)] + 1))
                weights(l, w0, 2 * C_POOL, "w_in", COL["c_gate"], C_ATT, "c_in")
                weights(l, w0, 0, "w_in", COL["b_val"], 2 * C_POOL, "b_in")
                for name, out, keep in (("state_conv", o_conv_s, TAIL - 1), ("state_pool", o_pool_s, POOL_BUF - 1)):
                    sp.dma_start(out[bass.ds(l, 1), :, 0:keep].rearrange("o s w c -> (o s) (w c)"),
                                 one(name, l)[:, :, 1:keep + 1].rearrange("o s w c -> (o s) (w c)"))\
                        .then_inc(S["state_out"], 16)
                bulk(COPIES_AFTER[l]["gates"])
                sp.wait_ge(S["ks_used"], nth(l, "ks_used", 1))
                gather("v", l, "v_in")
                sp.wait_ge(S["pj_full"], nth(l, "pj_full", PIDX[("v", AT - 1)] + 1))
                for h in range(2):
                    weights(l, w1, h * 512, "w_out", h * 512, 512, f"wo_{h}")
                if l < DEPTH - 1:
                    params(l + 1)
                    states(l + 1)
                bulk(COPIES_AFTER[l]["values"])
            bulk_rest()
            sp.wait_ge(bulk_out, 16 * (COPIES + 2))
            for name in ("v_out", "k_out", "new_out", "tail_out", "state_out"):
                sp.wait_ge(S[name], DEPTH * per[name])
            sp.wait_ge(y_out, 32)

        @block.gpsimd
        def _(pool):
            for name in (*START, *STAGED):
                pool.sem_inc(S[name], 1)
            for l in range(DEPTH):
                for step in SCHEDULE:
                    kind = step[0] if isinstance(step, tuple) else step
                    if kind == "gate":
                        e = GATES.index(PROJ[step[1]][0:2])
                        pool.wait_ge(S["exp_ok"], nth(l, "exp_ok", e + 1))
                        nc.gpsimd.tensor_scalar(ex[:, e % 2, :], ex[:, e % 2, :], LIMIT, 1.0, ALU.min, ALU.add).then_inc(S["clamp_ok"], 1)
                    elif kind == "sscore":
                        a, b = SCORE_CUTS[step[1]]
                        if step[1] == 0:
                            pool.wait_ge(S["k_in"], nth(l, "k_in", per["k_in"]))
                            pool.wait_ge(S["tr_free"], nth(l, "tr_free", TR["qb"] + 1))
                        nc.gpsimd.tensor_tensor(kv[:, a:b, :], kv[:, a:b, :], qb[:, None, :].to_broadcast([P, b - a, C_ATT]),
                                                ALU.mult).then_inc(S["kprod_ok"], 1)
                if l < DEPTH - 1:
                    for name, stored in STAGED.items():
                        pool.wait_ge(S[stored], nth(l, stored, per[stored]))
                        pool.sem_inc(S[name], 1)

        @block.tensor
        def _(pe):
            def turn(out, in_, rows):
                return nc.tensor.transpose(out, in_, C["ident"][0:rows, 0:rows])

            pe.wait_ge(early_in, 16)
            pe.wait_ge(x_in, 32)
            for u in range(XROUNDS):
                if u >= 2:
                    pe.wait_ge(x_copied, u - 1)
                out = (psc, po)[u % 2]
                if u < 4:
                    r, k0 = u // 2, 4 * (u % 2)
                    for k in range(4):
                        col = r * D_MODEL + (k0 + k) * P
                        last = turn(out[:, k * P:(k + 1) * P], x_tok[:, col:col + P], P)
                else:
                    for k in range(KD):
                        col = 2 * D_MODEL + k * P
                        last = turn(out[:, k * NS:(k + 1) * NS], x_tok[0:NS, col:col + P], NS)
                last.then_inc(x_turned, 1)

            def sum_squares(k):
                return nc.tensor.matmul(ps[:, 0:T], ones[:, :], hT[:, k, :], start=(k == 0), stop=(k == KD - 1))

            pe.wait_ge(diagonal_ok, 1)
            nc.tensor.matmul(ps[:, 0:P], ones[:, :], diagonal[:, 0:P], start=True, stop=True)
            nc.tensor.matmul(ps[:, P:SEQ], ones[:, :], diagonal[:, P:SEQ], start=True, stop=True)
            nc.tensor.matmul(ps[:, SEQ:T], ones[0:NS, :], diagonal[0:NS, SEQ:T], start=True, stop=True).then_inc(S["st_full"], 1)
            pe.wait_ge(const_in, 16)

            with pe.Fori(0, DEPTH) as l:
                def tr_use(step):
                    pe.wait_ge(S["tr_free"], nth(l, "tr_free", TR[step]))

                for step in SCHEDULE:
                    kind = step[0] if isinstance(step, tuple) else step
                    if kind == "par":
                        pe.wait_ge(S["par_in"], nth(l, "par_in", per["par_in"]))
                        tr_use(step)
                        turn(ptr[:, 0:ROWS], prow[:, :], ROWS).then_inc(S["tr_full"], 1)
                    elif kind == "st0":
                        pe.wait_ge(S["st_in"], nth(l, "st_in", per["st_in"]))
                        tr_use(step)
                        for t in range(2):
                            for r in range(2):
                                c = (2 * t + r) * 120
                                last = turn(ptr[:, c:c + 120], st_conv[:, r, t * P:(t + 1) * P], 120)
                        last.then_inc(S["tr_full"], 1)
                    elif kind == "st1":
                        tr_use(step)
                        for r in range(2):
                            turn(ptr[:, r * 120:r * 120 + 120], st_conv[:, r, 2 * P:3 * P], 120)
                        for t in range(PT_):
                            last = turn(ptr[:, 240 + t * 120:360 + t * 120], st_pool[:, t * P:(t + 1) * P], 120)
                        last.then_inc(S["tr_full"], 1)
                    elif kind == "proj":
                        n = step[1]
                        group, t, buf, col = PROJ[n]
                        if t == 0:
                            loaded = {"q": "q_in", "k": "k_w_in", "v": "v_w_in", "c_gate": "c_in", "b_val": "b_in",
                                      "b_gate": "b_in"}.get(group, f"{group}_in")
                            pe.wait_ge(S[loaded], nth(l, loaded, 16))
                        pe.wait_ge(S[f"pj_free{n % RING}"], nth(l, f"pj_free{n % RING}", n // RING))
                        for k in range(KD):
                            if n == 0:
                                pe.wait_ge(S["h_ok"], nth(l, "h_ok", k + 1))
                            last = nc.tensor.matmul(pj[n % RING][:, 0:T], wbuf[buf][:, k, col:col + P], hT[:, k, :],
                                                    start=(k == 0), stop=(k == KD - 1))
                        last.then_inc(S["pj_full"], 1)
                    elif kind == "norm":
                        i = step[1]
                        pe.wait_ge(S["qk_raw"], nth(l, "qk_raw", i + 1))
                        pe.wait_ge(S["st_free"], nth(l, "st_free", ST[step]))
                        nc.tensor.matmul(ps[:, 0:T], C["heads"], sq[:, i % 2, :], start=True, stop=True).then_inc(S["st_full"], 1)
                        pe.wait_ge(S["rt_free"], nth(l, "rt_free", i))
                        nc.tensor.matmul(prt[:, 0:T], C["rot"], qg[:, i % 2, :], start=True, stop=True).then_inc(S["rt_full"], 1)
                    elif kind in ("vtok", "ktok"):
                        j = step[1]
                        if kind == "vtok":
                            pe.wait_ge(S["v_raw"], nth(l, "v_raw", AT))
                        else:
                            pe.wait_ge(S["qk_ok"], nth(l, "qk_ok", 2 * AT))
                        tr_use(step)
                        for t in range(AT):
                            src = vT[:, t, j * P:(j + 1) * P] if kind == "vtok" else qk[:, AT + t, j * P:(j + 1) * P]
                            last = turn(ptr[:, t * P:(t + 1) * P], src, P)
                        last.then_inc(S["tr_full"], 1)
                    elif kind in ("qb", "kb", "vb"):
                        pe.wait_ge(S["rep_ok"], nth(l, "rep_ok", ("qb", "kb", "vb").index(kind) + 1))
                        pe.wait_ge(S["tr_free"], nth(l, "tr_free", TR[step]))
                        for t in range(AT):
                            last = turn(ptr[:, t * P:(t + 1) * P], rep[:, t, :], P)
                        last.then_inc(S["tr_full"], 1)
                    elif kind == "score":
                        h = step[1]
                        b = HD * (h % 2)
                        if h == 0:
                            pe.wait_ge(S["qk_ok"], nth(l, "qk_ok", 2 * AT))
                        pe.wait_ge(S["sc_free"], nth(l, "sc_free", h))
                        q, k = qk[b:b + HD, h // 2, :], qk[b:b + HD, AT + h // 2, :]
                        nc.tensor.matmul(psc[:, 0:P], q[:, 0:P], k[:, 0:P], start=True, stop=True)
                        nc.tensor.matmul(psc[:, P:3 * P], q[:, P:2 * P], k[:, 0:2 * P], start=True, stop=True)\
                            .then_inc(S["sc_full"], 1)
                    elif kind == "probT":
                        h = step[1]
                        pe.wait_ge(S["p_ok"], nth(l, "p_ok", h + 1))
                        tr_use(step)
                        for b in range(3):
                            last = turn(ptr[:, b * P:(b + 1) * P], sc[:, h % 2, b * P:(b + 1) * P], P)
                        last.then_inc(S["tr_full"], 1)
                    elif kind == "out":
                        h = step[1]
                        b = HD * (h % 2)
                        pe.wait_ge(S["tr_free"], nth(l, "tr_free", max(TR[("probT", h)], TR[("vtok", 1)]) + 1))
                        if h % 2 == 0:
                            pe.wait_ge(S["o_free"], nth(l, "o_free", h // 2))
                        v0, v1 = (v_tok[:, j, h * HD:(h + 1) * HD] for j in range(2))
                        p_ = pT[:, h % 2, :]
                        nc.tensor.matmul(po[b:b + HD, 0:P], v0, p_[:, 0:P], start=True, stop=True)
                        nc.tensor.matmul(po[b:b + HD, P:2 * P], v0, p_[:, P:2 * P], start=True, stop=False)
                        nc.tensor.matmul(po[b:b + HD, P:2 * P], v1, p_[:, 2 * P:3 * P], start=False, stop=True)\
                            .then_inc(S["o_full"], 1)
                    elif kind == "spv":
                        a, b = SV_CUTS[step[1]]
                        if a == 0:
                            pe.wait_ge(S["sc_free"], nth(l, "sc_free", NH))
                            pe.wait_ge(S["spm_ok"], nth(l, "spm_ok", 1))
                            pe.wait_ge(S["tr_free"], nth(l, "tr_free", TR["vb"] + 1))
                            pe.wait_ge(S["v_in"], nth(l, "v_in", per["v_in"]))
                        for j in range(a, b):
                            v = kv[:, j, :] if j < NEW else kvb[:, 1, :]
                            nc.tensor.matmul(psc[0:NH * NS, 0:C_ATT], spm[:, j * NH:(j + 1) * NH, :].rearrange("p h s -> p (h s)"), v,
                                             start=(j == 0), stop=(j == SLOTS))
                        if b == SLOTS + 1:
                            nc.tensor.matmul(psc[0:NH * NS, C_ATT:C_ATT + 1], spsum[:, :], ones[:, 0:1], start=True, stop=True)\
                                .then_inc(S["sc_full"], 1)
                    elif kind == "spT":
                        pe.wait_ge(S["so_ok"], nth(l, "so_ok", 1))
                        pe.wait_ge(S["tr_free"], nth(l, "tr_free", TR[step]))
                        for t in range(AT):
                            last = turn(ptr[:, t * P:(t + 1) * P], so[:, t * P:(t + 1) * P], P)
                        last.then_inc(S["tr_full"], 1)
                    elif kind == "poolw":
                        t = step[1]
                        if t == 0:
                            pe.wait_ge(S["pd_ok"], nth(l, "pd_ok", 1))
                            pe.wait_ge(S["pw_in"], nth(l, "pw_in", per["pw_in"]))
                        pe.wait_ge(S["rt_free"], nth(l, "rt_free", 2 * AT + t))
                        nc.tensor.matmul(prt[:, 0:T], pw[:, t, :], pd[:, t, :], start=True, stop=True).then_inc(S["rt_full"], 1)
                    elif kind == "conv_p":
                        pe.wait_ge(S["u_ok"], nth(l, "u_ok", CT))
                        pe.wait_ge(S["tr_free"], nth(l, "tr_free", TR[step]))
                        for t in range(CT):
                            last = turn(ptr[0:TAIL, t * P:(t + 1) * P], u_ext[:, t, SEQ:SEQ + TAIL], P)
                        last.then_inc(S["tr_full"], 1)
                    elif kind == "conv_s":
                        pe.wait_ge(S["tr_free"], nth(l, "tr_free", TR[step]))
                        for t in range(CT):
                            last = turn(ptr[0:NS, t * P:(t + 1) * P], u_smp[:, t, :, TAIL], P)
                        last.then_inc(S["tr_full"], 1)
                    elif kind == "pool_ps":
                        pe.wait_ge(S["b_val_ok"], nth(l, "b_val_ok", PT_))
                        pe.wait_ge(S["tr_free"], nth(l, "tr_free", TR[step]))
                        for t in range(PT_):
                            turn(ptr[0:POOL_BUF, t * P:(t + 1) * P], p_ext[:, t, SEQ:SEQ + POOL_BUF], P)
                            last = turn(ptr[0:NS, C_POOL + t * P:C_POOL + (t + 1) * P], p_smp[:, t, :, POOL_BUF], P)
                        last.then_inc(S["tr_full"], 1)
                    elif kind == "ln1":
                        pe.wait_ge(S["conv_ok"], nth(l, "conv_ok", CONV_TAPS))
                        pe.wait_ge(S["st_free"], nth(l, "st_free", ST[step]))
                        for t in range(CT):
                            last = nc.tensor.matmul(ps[:, 0:T], ones[:, :], yc[:, t, :], start=(t == 0), stop=(t == CT - 1))
                        last.then_inc(S["st_full"], 1)
                    elif kind == "ln2":
                        pe.wait_ge(S["ysq"], nth(l, "ysq", 1))
                        pe.wait_ge(S["st_free"], nth(l, "st_free", ST[step]))
                        for t in range(CT):
                            last = nc.tensor.matmul(ps[:, 0:T], ones[:, :], lns[:, t, :], start=(t == 0), stop=(t == CT - 1))
                        last.then_inc(S["st_full"], 1)
                    elif kind == "wout":
                        m = step[1]
                        n = NPROJ + m
                        if m % 4 == 0:
                            pe.wait_ge(S[f"wo_{m // 4}"], nth(l, f"wo_{m // 4}", 16))
                        pe.wait_ge(S[f"pj_free{n % RING}"], nth(l, f"pj_free{n % RING}", n // RING))
                        for k in range(KD):
                            if m == 0 and k == 0:
                                pe.wait_ge(S["mix_a"], nth(l, "mix_a", 1))
                            if m == 0 and k == CT + PT_:
                                pe.wait_ge(S["mix_c"], nth(l, "mix_c", AT))
                                pe.wait_ge(S["mix_s"], nth(l, "mix_s", 1))
                            if m == 0 and k == CT:
                                pe.wait_ge(S["mix_b"], nth(l, "mix_b", PT_))
                            last = nc.tensor.matmul(pj[n % RING][:, 0:T], w1[:, k, m * P:(m + 1) * P], mix[:, k, :],
                                                    start=(k == 0), stop=(k == KD - 1))
                        last.then_inc(S["pj_full"], 1)
                        if m == 1:
                            pe.wait_ge(S["st_free"], nth(l, "st_free", NST))
                        if m >= 1:
                            pe.wait_ge(S["xsq"], nth(l, "xsq", m))
                            sum_squares(m - 1)
                        if m == KD - 1:
                            pe.wait_ge(S["xsq"], nth(l, "xsq", KD))
                            sum_squares(m).then_inc(S["st_full"], 1)

            pe.wait_ge(S["xT_ok"], nth(DEPTH - 1, "xT_ok", KD))
            for u in range(XROUNDS):
                if u >= 2:
                    pe.wait_ge(y_copied, u - 1)
                out = (psc, po)[u % 2]
                r, k0 = u // 2, 4 * (u % 2)
                if u < 4:
                    for k in range(4):
                        last = turn(out[:, k * P:(k + 1) * P], xT[:, k0 + k, r * P:(r + 1) * P], P)
                    last.then_inc(y_turned, 1)
                else:
                    for k in range(4):
                        turn(out[0:NS, k * P:(k + 1) * P], xT[:, k, SEQ:T], P)
                    for k in range(4):
                        last = turn(ptr[0:NS, k * P:(k + 1) * P], xT[:, 4 + k, SEQ:T], P)
                    last.then_inc(y_turned, 1)

        @block.scalar
        def _(act):
            A = nc.scalar.activation
            nc.scalar.preload_act_table_set("natural_log_exp_and_others")
            act.wait_ge(x_in, 32)
            act.wait_ge(early_in, 16)
            unused = hT[:, :, :].rearrange("p k c -> p (k c)")
            for r in range(2):
                A(unused[:, r * D_MODEL:(r + 1) * D_MODEL], x_tok[:, r * D_MODEL:(r + 1) * D_MODEL], ACT.Square,
                  accum_out=x_sum[:, r:r + 1])
            A(mix[0:NS, :, :].rearrange("p k c -> p (k c)")[:, 0:D_MODEL], x_tok[0:NS, 2 * D_MODEL:3 * D_MODEL], ACT.Square,
              accum_out=x_sum[0:NS, 2:3]).then_inc(squared, 1)
            act.wait_ge(squared, 1)
            with act.Fori(0, DEPTH) as l:
                chain = [0]

                def link(ins):
                    chain[0] += 1
                    ins.then_inc(act_done, 1)
                    act.wait_ge(act_done, l * ACT_LINKS + chain[0])

                def rsqrt_of(dst, src, scale, free_n, ok_sem, n):
                    A(dst, src, ACT.Ln, scale=scale, bias=C["eps"]).then_inc(S["st_free"], 1)
                    act.wait_ge(S["st_free"], nth(l, "st_free", free_n))
                    A(dst, dst, ACT.Exp, scale=-0.5).then_inc(S[ok_sem], 1)
                    act.wait_ge(S[ok_sem], nth(l, ok_sem, n))

                for step in SCHEDULE:
                    kind = step[0] if isinstance(step, tuple) else step
                    if kind == "st0":
                        act.wait_ge(S["tr_full"], nth(l, "tr_full", TR[step] + 1))
                        nc.scalar.copy(u_smp[:, 0:2, :, 0:TAIL],
                                            ptr[:, 0:480].rearrange("p (t s w) -> p t s w", t=2, s=NS)).then_inc(S["tr_free"], 1)
                        act.wait_ge(S["tr_free"], nth(l, "tr_free", TR[step] + 1))
                    elif kind == "st1":
                        act.wait_ge(S["tr_full"], nth(l, "tr_full", TR[step] + 1))
                        nc.scalar.copy(u_smp[:, 2, :, 0:TAIL], ptr[:, 0:240].rearrange("p (s w) -> p s w", s=NS))
                        nc.scalar.copy(p_smp[:, :, :, 0:POOL_BUF],
                                            ptr[:, 240:480].rearrange("p (t s w) -> p t s w", t=2, s=NS)).then_inc(S["tr_free"], 1)
                        act.wait_ge(S["tr_free"], nth(l, "tr_free", TR[step] + 1))
                    elif kind == "rms":
                        act.wait_ge(S["st_full"], nth(l, "st_full", ST[step] + 1))
                        rsqrt_of(r_h[:, :], ps[:, 0:T], 1.0 / D_MODEL, ST[step] + 1, "r_h_ok", 1)
                    elif kind == "proj":
                        n = step[1]
                        group, t, _, _ = PROJ[n]
                        src = pj[n % RING][:, 0:T]
                        free = S[f"pj_free{n % RING}"]
                        act.wait_ge(S["pj_full"], nth(l, "pj_full", n + 1))
                        if group in "qk":
                            i = n - PIDX[("q", 0)]
                            if i >= 2:
                                act.wait_ge(S["qk_ok"], nth(l, "qk_ok", i - 1))
                            A(sq[:, i % 2, :], src, ACT.Square)
                            gain = par[:, ROW_QN:ROW_QN + 1] if group == "q" else par[:, ROW_KN:ROW_KN + 1]
                            if i == 0:
                                act.wait_ge(S["tr_free"], nth(l, "tr_free", TR["par"] + 1))
                            A(qg[:, i % 2, :], src, ACT.Copy, scale=gain).then_inc(S["qk_raw"], 1)
                            act.wait_ge(S["qk_raw"], nth(l, "qk_raw", i + 1))
                            act.sem_inc(free, 1)
                        elif group == "v":
                            nc.scalar.copy(vT[:, t, :], src).then_inc(S["v_raw"], 1)
                            act.wait_ge(S["v_raw"], nth(l, "v_raw", t + 1))
                            act.sem_inc(free, 1)
                        elif (group, t) in GATES:
                            e = GATES.index((group, t))
                            if e >= 2:
                                g2, t2 = GATES[e - 2]
                                act.wait_ge(S[GATE_USED[g2]], nth(l, GATE_USED[g2], t2 + 1))
                            A(ex[:, e % 2, :], src, ACT.Exp, scale=-1.0).then_inc(S["exp_ok"], 1)
                            act.wait_ge(S["exp_ok"], nth(l, "exp_ok", e + 1))
                            if group == "a_glu":
                                act.sem_inc(free, 1)
                        elif group == "b_val":
                            nc.scalar.copy(p_ext[:, t, POOL_BUF:], src[:, 0:SEQ])
                            nc.scalar.copy(p_smp[:, t, :, POOL_BUF], src[:, SEQ:T]).then_inc(S["b_val_ok"], 1)
                            act.wait_ge(S["b_val_ok"], nth(l, "b_val_ok", t + 1))
                            act.sem_inc(free, 1)
                    elif kind == "gate":
                        e = GATES.index(PROJ[step[1]][0:2])
                        act.wait_ge(S["clamp_ok"], nth(l, "clamp_ok", e + 1))
                        link(A(ex[:, e % 2, :], ex[:, e % 2, :], ACT.Ln))
                        A(ex[:, e % 2, :], ex[:, e % 2, :], ACT.Exp, scale=-1.0).then_inc(S["sig_ok"], 1)
                        act.wait_ge(S["sig_ok"], nth(l, "sig_ok", e + 1))
                    elif kind == "norm":
                        i = step[1]
                        act.wait_ge(S["st_full"], nth(l, "st_full", ST[step] + 1))
                        rsqrt_of(r_qk[:, i % 2, :], ps[:, 0:T], 1.0 / HD, ST[step] + 1, "qk_r", i + 1)
                    elif kind in ("vtok", "ktok"):
                        j = step[1]
                        tok, out, name = (v_tok, o_v_p, "v_out") if kind == "vtok" else (k_tok, o_k_p, "k_out")
                        if j == 0:
                            act.wait_ge(S[name[0] + "_staged"], nth(l, name[0] + "_staged", 0))
                        act.wait_ge(S["tr_full"], nth(l, "tr_full", TR[step] + 1))
                        nc.scalar.copy(tok[:, j, :], ptr[:, 0:C_ATT]).then_inc(S["tr_free"], 1)
                        act.wait_ge(S["tr_free"], nth(l, "tr_free", TR[step] + 1))
                        if j == 1:
                            act.dma_start(out[bass.ds(l, 1)].rearrange("l b (r p) h d -> p (l b r) (h d)", p=P),
                                          tok[:, :, :]).then_inc(S[name], 16)
                    elif kind in ("rep_q", "rep_k", "rep_v"):
                        if kind == "rep_q":
                            act.wait_ge(S["qk_ok"], nth(l, "qk_ok", AT))
                            i, src = 0, qk[:, 0:AT]
                        elif kind == "rep_k":
                            act.wait_ge(S["qk_ok"], nth(l, "qk_ok", 2 * AT))
                            act.wait_ge(S["tr_full"], nth(l, "tr_full", TR["qb"] + 1))
                            i, src = 1, qk[:, AT:2 * AT]
                        else:
                            act.wait_ge(S["tr_full"], nth(l, "tr_full", TR["kb"] + 1))
                            i, src = 2, vT[:, :]
                        nc.scalar.copy(rep[:, :, :].rearrange("p t (s a) -> p t s a", s=NS),
                                       src[:, :, SEQ:T, None].to_broadcast([P, AT, NS, PER_S])).then_inc(S["rep_ok"], 1)
                        act.wait_ge(S["rep_ok"], nth(l, "rep_ok", i + 1))
                    elif kind in ("kb", "vb"):
                        j = 0 if kind == "kb" else 1
                        if kind == "kb":
                            act.wait_ge(S["new_staged"], nth(l, "new_staged", 0))
                        act.wait_ge(S["tr_full"], nth(l, "tr_full", TR[step] + 1))
                        nc.scalar.copy(kvb[:, j, :], ptr[:, 0:C_ATT]).then_inc(S["tr_free"], 1)
                        act.wait_ge(S["tr_free"], nth(l, "tr_free", TR[step] + 1))
                        out = (o_k_s, o_v_s)[j]
                        act.dma_start(out[bass.ds(l, 1), :, PAST - 1].rearrange("l s h d -> (l s) (h d)"),
                                      kvb[0:P:PER_S, j, :]).then_inc(S["new_out"], 16)
                    elif kind == "pnorm":
                        h = step[1]
                        act.wait_ge(S["nmax_ok"], nth(l, "nmax_ok", h + 1))
                        A(sc[:, h % 2, 0:P], sc[:, h % 2, 0:P], ACT.Exp, bias=nmax[:, h % 2, 0:1],
                          accum_out=lsum[:, h % 2, 0:1])
                        A(sc[:, h % 2, P:3 * P], sc[:, h % 2, P:3 * P], ACT.Exp, bias=nmax[:, h % 2, 1:2],
                               accum_out=lsum[:, h % 2, 1:2]).then_inc(S["p_raw"], 1)
                        act.wait_ge(S["p_raw"], nth(l, "p_raw", h + 1))
                    elif kind == "probT":
                        h = step[1]
                        if h >= 2:
                            act.wait_ge(S["o_full"], nth(l, "o_full", h - 1))
                        act.wait_ge(S["tr_full"], nth(l, "tr_full", TR[step] + 1))
                        nc.scalar.copy(pT[:, h % 2, :], ptr[:, 0:3 * P]).then_inc(S["tr_free"], 1)
                        act.wait_ge(S["tr_free"], nth(l, "tr_free", TR[step] + 1))
                    elif kind == "ssoft1":
                        act.wait_ge(S["ssub"], nth(l, "ssub", 1))
                        A(spr[:, :, :], ssc[:, :, :], ACT.Exp).then_inc(S["sexp"], 1)
                        act.wait_ge(S["sexp"], nth(l, "sexp", 1))
                    elif kind in ("conv_p", "conv_s", "pool_ps"):
                        if kind == "conv_p":
                            act.wait_ge(S["tail_staged"], nth(l, "tail_staged", 0))
                        copies = {"conv_p": ((t_conv_p, ptr[0:TAIL, 0:C_CONV], o_conv_p, None),),
                                  "conv_s": ((t_conv_s, ptr[0:NS, 0:C_CONV], o_conv_s, TAIL - 1),),
                                  "pool_ps": ((t_pool_p, ptr[0:POOL_BUF, 0:C_POOL], o_pool_p, None),
                                              (t_pool_s, ptr[0:NS, C_POOL:2 * C_POOL], o_pool_s, POOL_BUF - 1))}[kind]
                        act.wait_ge(S["tr_full"], nth(l, "tr_full", TR[step] + 1))
                        for dst, src, _, _ in copies:
                            last = nc.scalar.copy(dst[:, :], src)
                        last.then_inc(S["tr_free"], 1)
                        act.wait_ge(S["tr_free"], nth(l, "tr_free", TR[step] + 1))
                        for dst, _, out, row in copies:
                            o = out[bass.ds(l, 1)].rearrange("l b w c -> (l b w) c") if row is None else \
                                out[bass.ds(l, 1), :, row].rearrange("l s c -> (l s) c")
                            act.dma_start(o, dst[:, :]).then_inc(S["tail_out"], 16)
                    elif kind == "ln1":
                        act.wait_ge(S["yc_ok"], nth(l, "yc_ok", 1))
                        A(lns, yc[:, :, :], ACT.Square).then_inc(S["ysq"], 1)
                        act.wait_ge(S["ysq"], nth(l, "ysq", 1))
                    elif kind == "ln2":
                        act.wait_ge(S["st_full"], nth(l, "st_full", ST[step] + 1))
                        rsqrt_of(r_h[:, :], ps[:, 0:T], 1.0 / C_CONV, ST[step] + 1, "rstd_ok", 1)
                    elif kind == "ln3":
                        act.wait_ge(S["z_ok"], nth(l, "z_ok", 1))
                        A(lns, yc[:, :, :], ACT.Exp, scale=-1.0).then_inc(S["zexp"], 1)
                        act.wait_ge(S["zclamp"], nth(l, "zclamp", 1))
                        link(A(lns, lns, ACT.Ln))
                        A(lns, lns, ACT.Exp, scale=-1.0).then_inc(S["zsig"], 1)
                        act.wait_ge(S["zsig"], nth(l, "zsig", 1))
                    elif kind == "wout":
                        m = step[1]
                        act.wait_ge(S["xT_ok"], nth(l, "xT_ok", m + 1))
                        A(hT[:, m, :], xT[:, m, :], ACT.Square).then_inc(S["xsq"], 1)
                        if m == KD - 1:
                            act.wait_ge(S["xsq"], nth(l, "xsq", KD))
                assert chain[0] == ACT_LINKS, chain[0]

            for u in range(XROUNDS):
                act.wait_ge(y_turned, u + 1)
                src = (psc, po)[u % 2]
                r, k0 = u // 2, 4 * (u % 2)
                if u < 4:
                    nc.scalar.copy(x_tok[:, r * D_MODEL + k0 * P:r * D_MODEL + (k0 + 4) * P], src[:, :]).then_inc(y_copied, 1)
                else:
                    nc.scalar.copy(x_tok[0:NS, 2 * D_MODEL:2 * D_MODEL + 512], src[0:NS, :])
                    nc.scalar.copy(x_tok[0:NS, 2 * D_MODEL + 512:3 * D_MODEL], ptr[0:NS, :]).then_inc(y_copied, 1)
            act.wait_ge(y_copied, XROUNDS)
            act.dma_start(y_prompt.rearrange("b (r p) d -> p (b r) d", p=P),
                          x_tok[:, 0:2 * D_MODEL].rearrange("p (r d) -> p r d", r=2)).then_inc(y_out, 16)
            act.dma_start(y_sample.rearrange("s t d -> (s t) d"), x_tok[0:NS, 2 * D_MODEL:3 * D_MODEL]).then_inc(y_out, 16)

        @block.vector
        def _(dve):
            V = nc.vector
            V.memset(ones[:, :], 1.0)
            V.memset(u_ext[:, :, 0:TAIL], 0.0)
            V.memset(p_ext[:, :, 0:POOL_BUF], 0.0)
            V.memset(mx[:, :, :], 0.0)
            V.memset(so[:, :], 0.0)
            V.memset(pw[:, :, :], 0.0).then_inc(zeroed, 1)
            dve.wait_ge(zeroed, 1)
            dve.wait_ge(early_in, 16)
            dve.wait_ge(squared, 1)
            for r in range(2):
                V.tensor_scalar(diagonal[:, r * P:(r + 1) * P], C["ident"], x_sum[:, r:r + 1], None, ALU.mult)
            V.tensor_scalar(diagonal[0:NS, SEQ:T], C["ident"][0:NS, 0:NS], x_sum[0:NS, 2:3], None, ALU.mult).then_inc(diagonal_ok, 1)
            dve.wait_ge(diagonal_ok, 1)
            dve.wait_ge(const_in, 16)
            for u in range(XROUNDS):
                dve.wait_ge(x_turned, u + 1)
                src = (psc, po)[u % 2]
                if u < 4:
                    r, k0 = u // 2, 4 * (u % 2)
                    V.tensor_copy(xT[:, k0:k0 + 4, r * P:(r + 1) * P], src[:, :].rearrange("p (k c) -> p k c", k=4))\
                        .then_inc(x_copied, 1)
                else:
                    V.tensor_copy(xT[:, :, SEQ:T], src[:, 0:KD * NS].rearrange("p (k c) -> p k c", k=KD)).then_inc(x_copied, 1)
            dve.wait_ge(x_copied, XROUNDS)

            with dve.Fori(0, DEPTH) as l:
                chain = [0]

                def link(ins):
                    chain[0] += 1
                    ins.then_inc(dve_done, 1)
                    dve.wait_ge(dve_done, l * DVE_LINKS + chain[0])

                def sigmoid(group, t):
                    e = GATES.index((group, t))
                    dve.wait_ge(S["sig_ok"], nth(l, "sig_ok", e + 1))
                    return ex[:, e % 2, :]

                for step in SCHEDULE:
                    kind = step[0] if isinstance(step, tuple) else step
                    if kind == "par":
                        dve.wait_ge(S["tr_full"], nth(l, "tr_full", TR[step] + 1))
                        V.tensor_copy(par[:, :], ptr[:, 0:ROWS]).then_inc(S["tr_free"], 1)
                        dve.wait_ge(S["tr_free"], nth(l, "tr_free", TR[step] + 1))
                    elif kind == "rms":
                        dve.wait_ge(S["r_h_ok"], nth(l, "r_h_ok", 1))
                        for k in range(KD):
                            V.scalar_tensor_tensor(out=hT[:, k, :], in0=xT[:, k, :], scalar=par[:, ROW_NG + k:ROW_NG + k + 1],
                                                   in1=r_h[:, :], op0=ALU.mult, op1=ALU.mult).then_inc(S["h_ok"], 1)
                        dve.wait_ge(S["h_ok"], nth(l, "h_ok", KD))
                    elif kind == "norm":
                        i = step[1]
                        dve.wait_ge(S["qk_raw"], nth(l, "qk_raw", i + 1))
                        V.tensor_tensor(roped[:, :], qg[:, i % 2, :], C["cos"], ALU.mult)
                        dve.wait_ge(S["rt_full"], nth(l, "rt_full", i + 1))
                        V.tensor_tensor(ropes[:, :], prt[:, 0:T], C["sin"], ALU.mult).then_inc(S["rt_free"], 1)
                        dve.wait_ge(S["rt_free"], nth(l, "rt_free", i + 1))
                        link(V.tensor_tensor(roped[:, :], roped[:, :], ropes[:, :], ALU.add))
                        dve.wait_ge(S["qk_r"], nth(l, "qk_r", i + 1))
                        V.tensor_tensor(qk[:, i, :], roped[:, :], r_qk[:, i % 2, :], ALU.mult).then_inc(S["qk_ok"], 1)
                        dve.wait_ge(S["qk_ok"], nth(l, "qk_ok", i + 1))
                    elif kind == "gate":
                        n = step[1]
                        group, t, _, _ = PROJ[n]
                        src = pj[n % RING][:, 0:T]
                        free = S[f"pj_free{n % RING}"]
                        if group == "a_glu":
                            s = sigmoid(group, t)
                            val = pj[(n - 1) % RING][:, 0:T]
                            V.tensor_tensor(u_ext[:, t, TAIL:], val[:, 0:SEQ], s[:, 0:SEQ], ALU.mult)
                            V.tensor_tensor(u_smp[:, t, :, TAIL], val[:, SEQ:T], s[:, SEQ:T], ALU.mult).then_inc(S["u_ok"], 1)
                            dve.wait_ge(S["u_ok"], nth(l, "u_ok", t + 1))
                            dve.sem_inc(S[f"pj_free{(n - 1) % RING}"], 1)
                        elif group in ("c_gate", "a_gate", "b_gate"):
                            dst, name = {"c_gate": (sig_c, "sig_c_ok"), "a_gate": (sig_a, "sig_a_ok"), "b_gate": (sig_b, "sig_b_ok")}[group]
                            s = sigmoid(group, t)
                            V.tensor_tensor(dst[:, t, :], src, s, ALU.mult).then_inc(S[name], 1)
                            dve.wait_ge(S[name], nth(l, name, t + 1))
                            dve.sem_inc(free, 1)
                    elif kind == "qb":
                        dve.wait_ge(S["tr_full"], nth(l, "tr_full", TR[step] + 1))
                        V.tensor_copy(qb[:, :], ptr[:, 0:C_ATT]).then_inc(S["tr_free"], 1)
                        dve.wait_ge(S["tr_free"], nth(l, "tr_free", TR[step] + 1))
                    elif kind == "score":
                        h = step[1]
                        dve.wait_ge(S["sc_full"], nth(l, "sc_full", h + 1))
                        if h >= 2:
                            dve.wait_ge(S["tr_full"], nth(l, "tr_full", TR[("probT", h - 2)] + 1))
                        V.scalar_tensor_tensor(out=sc[:, h % 2, :], in0=psc[:, 0:3 * P], scalar=SCALE, in1=C["bias"],
                                                    op0=ALU.mult, op1=ALU.add).then_inc(S["sc_free"], 1)
                        dve.wait_ge(S["sc_free"], nth(l, "sc_free", h + 1))
                        V.tensor_reduce(nmax[:, h % 2, 0:1], sc[:, h % 2, 0:P], AX.X, ALU.max, negate=True)
                        V.tensor_reduce(nmax[:, h % 2, 1:2], sc[:, h % 2, P:3 * P], AX.X, ALU.max, negate=True).then_inc(S["nmax_ok"], 1)
                        dve.wait_ge(S["nmax_ok"], nth(l, "nmax_ok", h + 1))
                    elif kind == "pnorm":
                        h = step[1]
                        dve.wait_ge(S["p_raw"], nth(l, "p_raw", h + 1))
                        link(V.reciprocal(rl[:, h % 2, :], lsum[:, h % 2, :]))
                        V.tensor_scalar(sc[:, h % 2, 0:P], sc[:, h % 2, 0:P], rl[:, h % 2, 0:1], None, ALU.mult)
                        V.tensor_scalar(sc[:, h % 2, P:3 * P], sc[:, h % 2, P:3 * P], rl[:, h % 2, 1:2], None, ALU.mult).then_inc(S["p_ok"], 1)
                        dve.wait_ge(S["p_ok"], nth(l, "p_ok", h + 1))
                    elif kind == "out":
                        h = step[1]
                        if h % 2:
                            t = h // 2
                            dve.wait_ge(S["o_full"], nth(l, "o_full", h + 1))
                            dve.wait_ge(S["sig_c_ok"], nth(l, "sig_c_ok", t + 1))
                            V.tensor_tensor(mix[:, CT + PT_ + t, 0:SEQ], po[:, 0:SEQ], sig_c[:, t, 0:SEQ], ALU.mult).then_inc(S["mix_c"], 1)
                            dve.wait_ge(S["mix_c"], nth(l, "mix_c", t + 1))
                            dve.sem_inc(S["o_free"], 1)
                    elif kind == "sscore":
                        i = step[1]
                        a, b = SCORE_CUTS[i]
                        dve.wait_ge(S["kprod_ok"], nth(l, "kprod_ok", i + 1))
                        last = V.tensor_reduce(ssc[:, a:b, :], kv[:, a:b, :].rearrange("p j (h d) -> p j h d", h=NH), AX.X, ALU.add)
                        if i == len(SCORE_CUTS) - 1:
                            last.then_inc(S["ks_used"], 1)
                            dve.wait_ge(S["ks_used"], nth(l, "ks_used", 1))
                        else:
                            link(last)
                    elif kind == "snew":
                        dve.wait_ge(S["tr_free"], nth(l, "tr_free", TR["kb"] + 1))
                        link(V.tensor_tensor(prod[:, :], kvb[:, 0, :], qb[:, :], ALU.mult))
                        link(V.tensor_reduce(ssc[:, NEW, :], prod[:, :].rearrange("p (h d) -> p h d", h=NH), AX.X, ALU.add))
                    elif kind == "ssoft0":
                        link(V.scalar_tensor_tensor(out=ssc[:, :, :], in0=ssc[:, :, :], scalar=SCALE,
                                                    in1=C["sbias"][:, :, None].to_broadcast([P, SLOTS + 1, NH]),
                                                    op0=ALU.mult, op1=ALU.add))
                        link(V.tensor_reduce(mx[:, 0, 0:NH], ssc[:, :, :].rearrange("p j h -> p h j"), AX.X, ALU.max))
                        link(V.transpose(mx[:, 1, :], mx[:, 0, :]))
                        link(V.tensor_reduce(mx2[:, :], mx[:, 1, :].rearrange("p (g a) -> p g a", g=2), AX.X, ALU.max))
                        link(V.tensor_copy(mx[:, 2, :].rearrange("p (g a) -> p g a", g=2), mx2[:, :, None].to_broadcast([P, 2, PER_S])))
                        link(V.transpose(mx[:, 3, :], mx[:, 2, :]))
                        V.tensor_tensor(ssc[:, :, :], ssc[:, :, :], mx[:, 3, None, 0:NH].to_broadcast([P, SLOTS + 1, NH]),
                                             ALU.subtract).then_inc(S["ssub"], 1)
                        dve.wait_ge(S["ssub"], nth(l, "ssub", 1))
                    elif kind == "ssoft1":
                        dve.wait_ge(S["sexp"], nth(l, "sexp", 1))
                        link(V.tensor_tensor(spm[:, :, :],
                                             spr[:, :, :].rearrange("p j h -> p (j h)")[:, :, None].to_broadcast([P, (SLOTS + 1) * NH, NS]),
                                             C["mask"][:, None, :].to_broadcast([P, (SLOTS + 1) * NH, NS]), ALU.mult))
                        V.tensor_reduce(spsum[:, :], spm[:, :, :].rearrange("p (j h) s -> p (h s) j", h=NH), AX.X, ALU.add).then_inc(S["spm_ok"], 1)
                        dve.wait_ge(S["spm_ok"], nth(l, "spm_ok", 1))
                    elif step == ("spv", len(SV_CUTS) - 1):
                        dve.wait_ge(S["sc_full"], nth(l, "sc_full", NH + 1))
                        rows = NH * NS
                        link(V.reciprocal(srl[:, :], psc[0:rows, C_ATT:C_ATT + 1]))
                        V.tensor_scalar(so[0:rows, :], psc[0:rows, 0:C_ATT], srl[:, :], None, ALU.mult).then_inc(S["so_ok"], 1)
                        dve.wait_ge(S["so_ok"], nth(l, "so_ok", 1))
                        dve.sem_inc(S["sc_free"], 1)
                    elif kind == "spT":
                        dve.wait_ge(S["tr_full"], nth(l, "tr_full", TR[step] + 1))
                        for t in range(AT):
                            for e in range(2):
                                b, c = HD * e, t * P + (2 * t + e) * NS
                                last = V.tensor_tensor(mix[b:b + HD, CT + PT_ + t, SEQ:T], ptr[b:b + HD, c:c + NS],
                                                       sig_c[b:b + HD, t, SEQ:T], ALU.mult)
                        last.then_inc(S["mix_s"], 1)
                        dve.wait_ge(S["mix_s"], nth(l, "mix_s", 1))
                        dve.sem_inc(S["tr_free"], 1)
                    elif kind == "conv":
                        for c in range(step[1], step[2]):
                            w, t = TAPS[c]
                            x_w = u_ext[:, t, w:w + SEQ]
                            if w == 0:
                                dve.wait_ge(S["u_ok"], nth(l, "u_ok", t + 1))
                                last = V.tensor_scalar(yc[:, t, 0:SEQ], x_w, par[:, ROW_CW + t:ROW_CW + t + 1],
                                                       par[:, ROW_CB + t:ROW_CB + t + 1], ALU.mult, ALU.add)
                            else:
                                dve.wait_ge(S["conv_ok"], nth(l, "conv_ok", TAPS.index((w - 1, t)) + 1))
                                last = V.scalar_tensor_tensor(out=yc[:, t, 0:SEQ], in0=x_w,
                                                              scalar=par[:, ROW_CW + w * CT + t:ROW_CW + w * CT + t + 1],
                                                              in1=yc[:, t, 0:SEQ], op0=ALU.mult, op1=ALU.add)
                            last.then_inc(S["conv_ok"], 1)
                    elif kind == "sconv":
                        for t in range(CT):
                            link(V.tensor_tensor(uw[:, :, :], u_smp[:, t, :, :], cw[:, t, None, :].to_broadcast([P, NS, CONV_W]), ALU.mult))
                            link(V.tensor_reduce(yc[:, t, SEQ:T], uw[:, :, :], AX.X, ALU.add))
                            link(V.tensor_scalar_add(yc[:, t, SEQ:T], yc[:, t, SEQ:T], par[:, ROW_CB + t:ROW_CB + t + 1]))
                    elif kind == "pool":
                        dve.wait_ge(S["b_val_ok"], nth(l, "b_val_ok", PT_))
                        L = POOL_BUF + SEQ
                        lo, hi = slice(0, 64), slice(64, P)
                        V.tensor_tensor(pd[lo, 0, 0:SEQ], p_ext[lo, 0, 15:L], p_ext[lo, 0, 14:L - 1], ALU.add)
                        link(V.tensor_tensor(pa[hi, 1:L], p_ext[hi, 0, 1:L], p_ext[hi, 0, 0:L - 1], ALU.add))
                        link(V.tensor_tensor(pd[hi, 0, 0:SEQ], pa[hi, 15:L], pa[hi, 13:L - 2], ALU.add))
                        link(V.tensor_tensor(pa[:, 1:L], p_ext[:, 1, 1:L], p_ext[:, 1, 0:L - 1], ALU.add))
                        link(V.tensor_tensor(pb[:, 3:L], pa[:, 3:L], pa[:, 1:L - 2], ALU.add))
                        V.tensor_tensor(pd[lo, 1, 0:SEQ], pb[lo, 15:L], pb[lo, 11:L - 4], ALU.add)
                        link(V.tensor_tensor(pa[hi, 7:L], pb[hi, 7:L], pb[hi, 3:L - 4], ALU.add))
                        V.tensor_tensor(pd[hi, 1, 0:SEQ], pa[hi, 15:L], pa[hi, 7:L - 8], ALU.add)
                        for g, w in enumerate(POOL_WINDOWS):
                            part = slice(64 * (g % 2), 64 * (g % 2) + 64)
                            last = V.tensor_reduce(pd[part, g // 2, SEQ:T], p_smp[part, g // 2, :, 16 - w:16], AX.X, ALU.add)
                        link(last)
                        n = POOL_BUF + 1
                        link(V.tensor_tensor(pd[:, :, 0:n], pd[:, :, 0:n], C["inv_cnt"].rearrange("p (t c) -> p t c", t=PT_), ALU.mult))
                        V.tensor_tensor(pd[:, :, 0:n], pd[:, :, 0:n], p_ext[:, :, POOL_BUF:POOL_BUF + n], ALU.subtract)
                        for t in range(PT_):
                            for cols, own in ((slice(n, SEQ), p_ext[:, t, POOL_BUF + n:]), (slice(SEQ, T), p_smp[:, t, :, POOL_BUF])):
                                last = V.scalar_tensor_tensor(out=pd[:, t, cols], in0=pd[:, t, cols], scalar=C["inv_win"][:, t:t + 1],
                                                              in1=own, op0=ALU.mult, op1=ALU.subtract)
                        last.then_inc(S["pd_ok"], 1)
                        dve.wait_ge(S["pd_ok"], nth(l, "pd_ok", 1))
                    elif kind == "poolw":
                        t = step[1]
                        dve.wait_ge(S["rt_full"], nth(l, "rt_full", 2 * AT + t + 1))
                        dve.wait_ge(S["sig_b_ok"], nth(l, "sig_b_ok", t + 1))
                        V.scalar_tensor_tensor(out=mix[:, CT + t, :], in0=prt[:, 0:T], scalar=par[:, ROW_PS + t:ROW_PS + t + 1],
                                               in1=sig_b[:, t, :], op0=ALU.mult, op1=ALU.mult).then_inc(S["mix_b"], 1)
                        dve.wait_ge(S["mix_b"], nth(l, "mix_b", t + 1))
                        dve.sem_inc(S["rt_free"], 1)
                    elif kind == "ln1":
                        dve.wait_ge(S["st_full"], nth(l, "st_full", ST[step] + 1))
                        V.scalar_tensor_tensor(out=yc[:, :, :], in0=ps[:, None, 0:T].to_broadcast([P, CT, T]), scalar=-1.0 / C_CONV,
                                               in1=yc[:, :, :], op0=ALU.mult, op1=ALU.add).then_inc(S["yc_ok"], 1)
                        dve.wait_ge(S["yc_ok"], nth(l, "yc_ok", 1))
                        dve.sem_inc(S["st_free"], 1)
                    elif kind == "ln2":
                        dve.wait_ge(S["rstd_ok"], nth(l, "rstd_ok", 1))
                        link(V.tensor_tensor(yc[:, :, :], yc[:, :, :], r_h[:, None, :].to_broadcast([P, CT, T]), ALU.mult))
                        for t in range(CT):
                            last = V.tensor_scalar(yc[:, t, :], yc[:, t, :], par[:, ROW_LG + t:ROW_LG + t + 1],
                                                   par[:, ROW_LB + t:ROW_LB + t + 1], ALU.mult, ALU.add)
                        last.then_inc(S["z_ok"], 1)
                        dve.wait_ge(S["z_ok"], nth(l, "z_ok", 1))
                        link(V.tensor_tensor(sig_a[:, :, :], sig_a[:, :, :], yc[:, :, :], ALU.mult))
                    elif kind == "ln3":
                        dve.wait_ge(S["zexp"], nth(l, "zexp", 1))
                        V.tensor_scalar(lns, lns, LIMIT, 1.0, ALU.min, ALU.add).then_inc(S["zclamp"], 1)
                        dve.wait_ge(S["zclamp"], nth(l, "zclamp", 1))
                        dve.wait_ge(S["zsig"], nth(l, "zsig", 1))
                        V.tensor_tensor(mix[:, 0:CT, :], sig_a[:, :, :], lns, ALU.mult).then_inc(S["mix_a"], 1)
                        dve.wait_ge(S["mix_a"], nth(l, "mix_a", 1))
                    elif kind == "wout":
                        m = step[1]
                        n = NPROJ + m
                        dve.wait_ge(S["pj_full"], nth(l, "pj_full", n + 1))
                        V.tensor_tensor(xT[:, m, :], xT[:, m, :], pj[n % RING][:, 0:T], ALU.add).then_inc(S["xT_ok"], 1)
                        dve.wait_ge(S["xT_ok"], nth(l, "xT_ok", m + 1))
                        dve.sem_inc(S[f"pj_free{n % RING}"], 1)
                assert chain[0] == DVE_LINKS, chain[0]


DVE_LINKS = 44
ACT_LINKS = 12

_INS = ["x_prompt", "x_sample", "state_conv", "state_pool", "cache_k_win", "cache_v_win", "norm_g", "w_in", "conv_w",
        "conv_b", "ln_g", "ln_b", "pool_w", "pool_scale", "q_norm_g", "k_norm_g", "w_out"]
_OUTS = [(1, SEQ, D_MODEL), (NS, 1, D_MODEL), (DEPTH, 1, TAIL, C_CONV), (DEPTH, 1, POOL_BUF, C_POOL),
         (DEPTH, 1, SEQ, NH, HD), (DEPTH, 1, SEQ, NH, HD), (DEPTH, NS, TAIL, C_CONV), (DEPTH, NS, POOL_BUF, C_POOL),
         (DEPTH, NS, PAST, NH, HD), (DEPTH, NS, PAST, NH, HD)]


def kernel(**inputs):
    import concourse.bacc as bacc
    from concourse.bass_utils import run_bass_kernel_spmd as run

    nc = bacc.Bacc("TRN2", target_bir_lowering=False, num_devices=1, dynamic_dma_scratch_size=1024)
    arrays, ins = {}, {}
    for name in _INS:
        a = np.ascontiguousarray(inputs[name])
        arrays[f"in_{name}"] = a
        ins[name] = nc.dram_tensor(f"in_{name}", a.shape, F32, kind="ExternalInput").ap()
    at, table = constants()
    arrays["in_const"] = table
    const = nc.dram_tensor("in_const", table.shape, F32, kind="ExternalInput").ap()
    outs = [nc.dram_tensor(f"out_{i}", s, F32, kind="ExternalOutput").ap() for i, s in enumerate(_OUTS)]
    trunk_program(nc, ins, const, at, outs)
    r = run(nc, [arrays], core_ids=[0])
    return tuple(r.results[0][f"out_{i}"] for i in range(len(_OUTS)))
```
